# Optimizing a Trainium2 kernel written in Bass

```python
import jax
import jax.numpy as jnp
from jax import lax
import numpy as np

D_MODEL = 1024
BATCH = 1
SEQ = 256
DEPTH = 1
DEC_BATCH = 8
DEC_SEQ = 4
PAST_LEN = 2048
PAGE_SIZE = 128

HEAD_DIM = 64
ROPE_DIM = HEAD_DIM // 4
ROPE_THETA = 500000.0
SWA_Q_HEADS = 8
SWA_KV_HEADS = 2
SWA_WINDOW = 128
DIL_PAIRS = ((128, 1), (512, 4), (2048, 16))
DIL_KV_HEADS = 4
DIL_Q_HEADS = DIL_KV_HEADS * len(DIL_PAIRS)
DIL_MAX_WINDOW = 2048
MEM_TOKENS = 256
MEM_HEADS = 4
N_BRANCHES = 3
N_EXPERTS = 32
TOP_K = 4
D_FF = D_MODEL
SWIGLU_LIMIT = 7.0
SWIGLU_ALPHA = 1.702
BLOCK = 128
MOE_BLOCK = 128
RMS_EPS = 1e-5
IN_SPLITS = (SWA_Q_HEADS * HEAD_DIM, SWA_KV_HEADS * HEAD_DIM, SWA_KV_HEADS * HEAD_DIM,
             DIL_Q_HEADS * HEAD_DIM, DIL_KV_HEADS * HEAD_DIM, DIL_KV_HEADS * HEAD_DIM,
             MEM_HEADS * HEAD_DIM, N_BRANCHES * D_MODEL)
IN_WIDTH = sum(IN_SPLITS)

kernel_name = 'hybrid_swa_dilated_mem_moe_step'

def rmsnorm(x, g):
    xf = x.astype(jnp.float32)
    y = xf * lax.rsqrt(jnp.mean(xf * xf, axis=-1, keepdims=True) + RMS_EPS)
    return (y * g.astype(jnp.float32)).astype(x.dtype)

def partial_rope(x, pos):
    half = ROPE_DIM // 2
    inv_freq = ROPE_THETA ** (-jnp.arange(half, dtype=jnp.float32) / half)
    ang = pos.astype(jnp.float32)[:, None] * inv_freq[None, :]
    cos = jnp.cos(ang)[:, None, :]
    sin = jnp.sin(ang)[:, None, :]
    xr = x[..., :ROPE_DIM].astype(jnp.float32)
    x1, x2 = xr[..., :half], xr[..., half:]
    rot = jnp.concatenate([x1 * cos - x2 * sin, x2 * cos + x1 * sin], axis=-1).astype(x.dtype)
    return jnp.concatenate([rot, x[..., ROPE_DIM:]], axis=-1)

def softmax_lse(s, sink=None):
    m = jnp.max(s, axis=-1, keepdims=True)
    if sink is not None:
        m = jnp.maximum(m, sink)
    e = jnp.exp(s - m)
    den = jnp.sum(e, axis=-1, keepdims=True)
    if sink is not None:
        den = den + jnp.exp(sink - m)
    return e / den, (m + jnp.log(den))[..., 0]

def banded_attention(q, k, v, max_dist, sink=None):
    B, L, Hq, D = q.shape
    Hkv = k.shape[2]
    G = Hq // Hkv
    T = BLOCK
    nb = -(-L // T)
    pad = nb * T - L
    qp = jnp.pad(q, ((0, 0), (0, pad), (0, 0), (0, 0)))
    kp = jnp.pad(k, ((0, 0), (T, pad), (0, 0), (0, 0)))
    vp = jnp.pad(v, ((0, 0), (T, pad), (0, 0), (0, 0)))
    qb = qp.reshape(B, nb, T, Hkv, G, D)
    kb = kp.reshape(B, nb + 1, T, Hkv, D)
    vb = vp.reshape(B, nb + 1, T, Hkv, D)
    kk = jnp.concatenate([kb[:, :-1], kb[:, 1:]], axis=2)
    vv = jnp.concatenate([vb[:, :-1], vb[:, 1:]], axis=2)
    qi = jnp.arange(T)[:, None] + T
    kj = jnp.arange(2 * T)[None, :]
    dist = qi - kj
    key_abs = jnp.arange(nb)[:, None, None] * T - T + kj[None]
    valid = (dist >= 0) & (dist <= max_dist) & (key_abs >= 0)
    s = jnp.einsum('bnqhgd,bnkhd->bnhgqk', qb, kk).astype(jnp.float32) * (HEAD_DIM ** -0.5)
    s = jnp.where(valid[None, :, None, None], s, -jnp.inf)
    p, lse = softmax_lse(s, sink)
    o = jnp.einsum('bnhgqk,bnkhd->bnqhgd', p.astype(v.dtype), vv).reshape(B, nb * T, Hq, D)[:, :L]
    lse = lse.transpose(0, 1, 4, 2, 3).reshape(B, nb * T, Hq)[:, :L]
    return o, lse

def gathered_attention(q, k_ext, v_ext, idx, sink=None):
    B, nq, Hq, D = q.shape
    Hkv = k_ext.shape[2]
    G = Hq // Hkv
    valid = idx >= 0
    safe = jnp.maximum(idx, 0)
    kg = k_ext[:, safe]
    vg = v_ext[:, safe]
    s = jnp.einsum('bqhgd,bqkhd->bhgqk', q.reshape(B, nq, Hkv, G, D), kg).astype(jnp.float32) * (HEAD_DIM ** -0.5)
    s = jnp.where(valid, s, -jnp.inf)
    p, lse = softmax_lse(s, sink)
    o = jnp.einsum('bhgqk,bqkhd->bqhgd', p.astype(v_ext.dtype), vg).reshape(B, nq, Hq, D)
    return o, lse.transpose(0, 3, 1, 2).reshape(B, nq, Hq)

def memory_attention(q, mk, mv):
    s = jnp.einsum('bqhd,bkhd->bhqk', q, mk).astype(jnp.float32) * (HEAD_DIM ** -0.5)
    p = jax.nn.softmax(s, axis=-1).astype(mv.dtype)
    return jnp.einsum('bhqk,bkhd->bqhd', p, mv)

def memory_kv(mem, g, w):
    B, M, _ = mem.shape
    mk, mv = jnp.split(rmsnorm(mem, g) @ w, 2, axis=-1)
    return mk.reshape(B, M, MEM_HEADS, HEAD_DIM), mv.reshape(B, M, MEM_HEADS, HEAD_DIM)

def _to_classes(t, dil):
    B, L = t.shape[:2]
    t = t.reshape((B, L // dil, dil) + t.shape[2:])
    return jnp.swapaxes(t, 1, 2).reshape((B * dil, L // dil) + t.shape[3:])

def _from_classes(t, dil, B):
    t = jnp.swapaxes(t.reshape((B, dil) + t.shape[1:]), 1, 2)
    return t.reshape((B, t.shape[1] * dil) + t.shape[3:])

def combine_dilations(outs, lses):
    alpha = jax.nn.softmax(jnp.stack(lses, axis=0), axis=0)
    o = jnp.stack(outs, axis=0).astype(jnp.float32)
    return jnp.sum(alpha[..., None] * o, axis=0).astype(outs[0].dtype)

def dilated_prompt(q, k, v):
    B = q.shape[0]
    outs, lses = [], []
    for g, (window, dil) in enumerate(DIL_PAIRS):
        qg = q[:, :, g * DIL_KV_HEADS:(g + 1) * DIL_KV_HEADS]
        o, lse = banded_attention(_to_classes(qg, dil), _to_classes(k, dil), _to_classes(v, dil), window // dil)
        outs.append(_from_classes(o, dil, B))
        lses.append(_from_classes(lse, dil, B))
    return combine_dilations(outs, lses)

def dilated_sample(q, k_ext, v_ext, n_past):
    qi = n_past + jnp.arange(q.shape[1])[:, None]
    outs, lses = [], []
    for g, (window, dil) in enumerate(DIL_PAIRS):
        idx = qi - dil * jnp.arange(window // dil + 1)[None, :]
        o, lse = gathered_attention(q[:, :, g * DIL_KV_HEADS:(g + 1) * DIL_KV_HEADS], k_ext, v_ext, idx)
        outs.append(o)
        lses.append(lse)
    return combine_dilations(outs, lses)

def project_inputs(x, norm_g, w_in, pos):
    B, L, _ = x.shape
    h = rmsnorm(x, norm_g)
    qa, ka, va, qb, kb, vb, qc, gate_logits = jnp.split(h @ w_in, np.cumsum(IN_SPLITS)[:-1].tolist(), axis=-1)
    heads = lambda t: t.reshape(B, L, -1, HEAD_DIM)
    return (partial_rope(heads(qa), pos), partial_rope(heads(ka), pos), heads(va),
            partial_rope(heads(qb), pos), partial_rope(heads(kb), pos), heads(vb),
            heads(qc), gate_logits)

def moe_ffn(h, w_router, b_router, w_gate_up, b_gate_up, w_down, b_down):
    shp = h.shape
    x2 = h.reshape(-1, D_MODEL)
    T = x2.shape[0]
    logits = (x2 @ w_router).astype(jnp.float32) + b_router.astype(jnp.float32)
    top_val, top_idx = lax.top_k(logits, TOP_K)
    gate = jax.nn.softmax(top_val, axis=-1)
    n_assign = T * TOP_K
    flat_e = top_idx.reshape(-1)
    order = jnp.argsort(flat_e)
    sorted_e = flat_e[order]
    sorted_tok = order // TOP_K
    sorted_gate = gate.reshape(-1)[order]
    counts = jnp.bincount(flat_e, length=N_EXPERTS)
    padded = (counts + MOE_BLOCK - 1) // MOE_BLOCK * MOE_BLOCK
    start = jnp.cumsum(counts) - counts
    pend = jnp.cumsum(padded)
    pstart = pend - padded
    dest = pstart[sorted_e] + jnp.arange(n_assign) - start[sorted_e]
    n_blocks = (n_assign + N_EXPERTS * (MOE_BLOCK - 1) + MOE_BLOCK - 1) // MOE_BLOCK
    row_tok = jnp.zeros((n_blocks * MOE_BLOCK,), jnp.int32).at[dest].set(sorted_tok.astype(jnp.int32))
    block_e = jnp.minimum(jnp.searchsorted(pend, jnp.arange(n_blocks) * MOE_BLOCK, side='right'), N_EXPERTS - 1)

    def expert_block(args):
        tok, e = args
        xb = x2[tok]
        gu = xb @ w_gate_up[e] + b_gate_up[e]
        gt = jnp.minimum(gu[:, :D_FF], SWIGLU_LIMIT)
        up = jnp.clip(gu[:, D_FF:], -SWIGLU_LIMIT, SWIGLU_LIMIT)
        glu = gt * jax.nn.sigmoid(gt * SWIGLU_ALPHA)
        return ((up + 1.0) * glu) @ w_down[e] + b_down[e]

    y_rows = lax.map(expert_block, (row_tok.reshape(n_blocks, MOE_BLOCK), block_e)).reshape(-1, D_MODEL)
    contrib = y_rows[dest] * sorted_gate[:, None].astype(y_rows.dtype)
    return jnp.zeros_like(x2).at[sorted_tok].add(contrib).reshape(shp)

def merge_and_ffn(x, oa, ob, oc, gate_logits, w_br_a, w_br_b, w_br_c, w_out, norm_ffn,
                  w_router, b_router, w_gate_up, b_gate_up, w_down, b_down):
    B, L, _ = x.shape
    g = jax.nn.sigmoid(gate_logits.astype(jnp.float32)).astype(x.dtype).reshape(B, L, N_BRANCHES, D_MODEL)
    merged = (g[:, :, 0] * (oa.reshape(B, L, -1) @ w_br_a)
              + g[:, :, 1] * (ob.reshape(B, L, -1) @ w_br_b)
              + g[:, :, 2] * (oc.reshape(B, L, -1) @ w_br_c))
    x = x + merged @ w_out
    return x + moe_ffn(rmsnorm(x, norm_ffn), w_router, b_router, w_gate_up, b_gate_up, w_down, b_down)

def setup_inputs(seed: int = 0) -> dict:
    key = jax.random.key(seed)
    ks = jax.random.split(key, 26)
    f32 = jnp.float32

    def nrm(k, shape, scale):
        return jax.random.normal(k, shape, f32) * scale

    def gain(k, shape):
        return 1.0 + 0.05 * jax.random.normal(k, shape, f32)

    d = D_MODEL
    la = min(SWA_WINDOW, PAST_LEN)
    lb = min(DIL_MAX_WINDOW, PAST_LEN)
    kva = (DEPTH, DEC_BATCH, la, SWA_KV_HEADS, HEAD_DIM)
    kvb = (DEPTH, DEC_BATCH, lb, DIL_KV_HEADS, HEAD_DIM)
    kvm = (DEPTH, DEC_BATCH, MEM_TOKENS, MEM_HEADS, HEAD_DIM)
    wa = SWA_Q_HEADS * HEAD_DIM
    wb = DIL_KV_HEADS * HEAD_DIM
    wc = MEM_HEADS * HEAD_DIM
    return {
        'x_prompt': nrm(ks[0], (BATCH, SEQ, d), 1.0),
        'x_sample': nrm(ks[1], (DEC_BATCH, DEC_SEQ, d), 1.0),
        'cache_swa_k': nrm(ks[2], kva, 1.0),
        'cache_swa_v': nrm(ks[3], kva, 1.0),
        'cache_dil_k': nrm(ks[4], kvb, 1.0),
        'cache_dil_v': nrm(ks[5], kvb, 1.0),
        'cache_mem_k': nrm(ks[6], kvm, 1.0),
        'cache_mem_v': nrm(ks[7], kvm, 1.0),
        'mem_prompt': nrm(ks[8], (BATCH, MEM_TOKENS, d), 1.0),
        'norm_attn': gain(ks[9], (DEPTH, d)),
        'norm_mem': gain(ks[10], (DEPTH, d)),
        'w_in': nrm(ks[11], (DEPTH, d, IN_WIDTH), d ** -0.5),
        'w_mem_kv': nrm(ks[12], (DEPTH, d, 2 * wc), d ** -0.5),
        'sinks': nrm(ks[13], (DEPTH, SWA_Q_HEADS), 0.5),
        'w_br_a': nrm(ks[14], (DEPTH, wa, d), wa ** -0.5),
        'w_br_b': nrm(ks[15], (DEPTH, wb, d), wb ** -0.5),
        'w_br_c': nrm(ks[16], (DEPTH, wc, d), wc ** -0.5),
        'w_out': nrm(ks[17], (DEPTH, d, d), d ** -0.5),
        'norm_ffn': gain(ks[18], (DEPTH, d)),
        'w_router': nrm(ks[19], (DEPTH, d, N_EXPERTS), d ** -0.5),
        'b_router': nrm(ks[20], (DEPTH, N_EXPERTS), 0.01),
        'w_gate_up': nrm(ks[21], (DEPTH, N_EXPERTS, d, 2 * D_FF), d ** -0.5),
        'b_gate_up': nrm(ks[22], (DEPTH, N_EXPERTS, 2 * D_FF), 0.01),
        'w_down': nrm(ks[23], (DEPTH, N_EXPERTS, D_FF, d), D_FF ** -0.5),
        'b_down': nrm(ks[24], (DEPTH, N_EXPERTS, d), 0.01),
        'norm_final': gain(ks[25], (d,)),
    }

def reference(x_prompt, x_sample, cache_swa_k, cache_swa_v, cache_dil_k, cache_dil_v, cache_mem_k, cache_mem_v,
              mem_prompt, norm_attn, norm_mem, w_in, w_mem_kv, sinks, w_br_a, w_br_b, w_br_c, w_out, norm_ffn,
              w_router, b_router, w_gate_up, b_gate_up, w_down, b_down, norm_final):
    n_prompt = x_prompt.shape[1]
    n_new = x_sample.shape[1]
    pos_p = jnp.arange(n_prompt, dtype=jnp.int32)
    pos_s = PAST_LEN + jnp.arange(n_new, dtype=jnp.int32)
    la = cache_swa_k.shape[2]
    lb = cache_dil_k.shape[2]
    la_p = min(SWA_WINDOW, n_prompt)
    lb_p = min(DIL_MAX_WINDOW, n_prompt)
    xp, xs = x_prompt, x_sample
    swa_k_p, swa_v_p, dil_k_p, dil_v_p, mem_k_p, mem_v_p = [], [], [], [], [], []
    swa_k_s, swa_v_s, dil_k_s, dil_v_s = [], [], [], []
    for l in range(DEPTH):
        sink = sinks[l].reshape(SWA_KV_HEADS, -1, 1, 1).astype(jnp.float32)
        ffn_w = (w_br_a[l], w_br_b[l], w_br_c[l], w_out[l], norm_ffn[l],
                 w_router[l], b_router[l], w_gate_up[l], b_gate_up[l], w_down[l], b_down[l])
        qa, ka, va, qb, kb, vb, qc, gl = project_inputs(xp, norm_attn[l], w_in[l], pos_p)
        mk, mv = memory_kv(mem_prompt, norm_mem[l], w_mem_kv[l])
        oa, _ = banded_attention(qa, ka, va, SWA_WINDOW - 1, sink)
        ob = dilated_prompt(qb, kb, vb)
        oc = memory_attention(qc, mk, mv)
        xp = merge_and_ffn(xp, oa, ob, oc, gl, *ffn_w)
        swa_k_p.append(ka[:, n_prompt - la_p:])
        swa_v_p.append(va[:, n_prompt - la_p:])
        dil_k_p.append(kb[:, n_prompt - lb_p:])
        dil_v_p.append(vb[:, n_prompt - lb_p:])
        mem_k_p.append(mk)
        mem_v_p.append(mv)
        qa, ka, va, qb, kb, vb, qc, gl = project_inputs(xs, norm_attn[l], w_in[l], pos_s)
        ka_ext = jnp.concatenate([cache_swa_k[l], ka], axis=1)
        va_ext = jnp.concatenate([cache_swa_v[l], va], axis=1)
        kb_ext = jnp.concatenate([cache_dil_k[l], kb], axis=1)
        vb_ext = jnp.concatenate([cache_dil_v[l], vb], axis=1)
        idx_a = la + jnp.arange(n_new)[:, None] - jnp.arange(SWA_WINDOW)[None, :]
        oa, _ = gathered_attention(qa, ka_ext, va_ext, idx_a, sink)
        ob = dilated_sample(qb, kb_ext, vb_ext, lb)
        oc = memory_attention(qc, cache_mem_k[l], cache_mem_v[l])
        xs = merge_and_ffn(xs, oa, ob, oc, gl, *ffn_w)
        swa_k_s.append(ka_ext[:, n_new:])
        swa_v_s.append(va_ext[:, n_new:])
        dil_k_s.append(kb_ext[:, n_new:])
        dil_v_s.append(vb_ext[:, n_new:])
    y_prompt = rmsnorm(xp, norm_final)
    y_sample = rmsnorm(xs, norm_final)
    return (y_prompt, y_sample,
            jnp.stack(swa_k_p), jnp.stack(swa_v_p), jnp.stack(dil_k_p), jnp.stack(dil_v_p),
            jnp.stack(mem_k_p), jnp.stack(mem_v_p),
            jnp.stack(swa_k_s), jnp.stack(swa_v_s), jnp.stack(dil_k_s), jnp.stack(dil_v_s))


_drawn_inputs = setup_inputs


def setup_inputs(seed=0):
    import zlib

    import numpy as np

    out = dict(_drawn_inputs(seed))
    spreads = {}
    factors = {'sinks': 8.0, 'b_gate_up': 8.0, 'b_down': 8.0}
    for name, (base, spread) in spreads.items():
        noise = np.random.default_rng([zlib.crc32(name.encode()), seed]).standard_normal(out[name].shape)
        drawn = base * np.exp(spread * noise) if base else spread * noise
        out[name] = jnp.asarray(drawn.astype(out[name].dtype))
    for name, factor in factors.items():
        out[name] = (out[name] * factor).astype(out[name].dtype)
    return out
```

```python
from contextlib import ExitStack

import numpy as np

import concourse.bass as bass
from concourse import mybir

F32 = mybir.dt.float32
BF16 = mybir.dt.bfloat16
I32 = mybir.dt.int32
U32 = mybir.dt.uint32
ALU = mybir.AluOpType
ACT = mybir.ActivationFunctionType
AX = mybir.AxisListType

P = 128
D = 1024
KC = D // P
SEQ = 256
NB_S, NQ_S = 8, 4
NS = NB_S * NQ_S
PAST = 2048
HD = 64
NTOK = [P, P, NS]
TOK0 = [0, P, 2 * P]
TT = SEQ + NS
WIN_A = 128
GROUPS = ((128, 1), (512, 4), (2048, 16))
NE = 32
TOPK = 4
BT = 64
NOV = (TT * TOPK) // BT
NBLK = NE + NOV
EPS = 1e-5
LIMIT = 7.0
ALPHA = 1.702
QSCALE = HD ** -0.5
NEG = -1e30
LB, LA, LM = 2048, 128, 256
NKR = 7
GATE0 = 2304
NSM_B = 512 + 512 + 128 + 3 * NS
NSM_A = LA + NS


def constants():
    cols, at = [], {}

    def put(name, a):
        a = np.asarray(a, np.float32).reshape(P, -1)
        at[name] = (sum(c.shape[1] for c in cols), a.shape[1])
        cols.append(a)

    p = np.arange(P)
    put("ident", np.eye(P))
    put("tri", (p[:, None] < p[None, :]))
    put("tri_incl", (p[:, None] <= p[None, :]))
    put("ones", np.ones((P, P)))
    key = np.arange(SEQ)
    dist = (P + p)[:, None] - key[None, :]
    put("mask_a", np.where((dist >= 0) & (dist < WIN_A), 0, NEG))
    put("mask_b", np.stack([np.where((dist >= 0) & (dist <= w) & (dist % d == 0), 0, NEG)
                            for w, d in GROUPS], 1))
    b, i = p // NQ_S % NB_S, p % NQ_S
    new_b, new_i = np.arange(NS) // NQ_S, np.arange(NS) % NQ_S
    same = b[:, None] == new_b
    before = new_i <= i[:, None]
    itself = new_i == i[:, None]
    put("smask_a", np.where(np.concatenate([np.arange(LA) > i[:, None], same & before], 1), 0, NEG))
    recent = 1536 + np.arange(512)
    far = np.arange(384) // 4 * 16 + np.arange(384) % 4
    near = 1536 + np.arange(128) // 4 * 16 + np.arange(128) % 4
    q = PAST + i[:, None]
    put("smask_b", np.where(np.concatenate([
        ((q - recent) % 4 == 0) & (q - recent <= 512),
        ((q - np.concatenate([far, near])) % 16 == 0) & (q - np.concatenate([far, near]) <= 2048),
        q - recent[384:] <= 128,
        same & before, same & itself, same & itself], 1), 0, NEG))
    half = HD // 8
    inv = np.float32(500000.0) ** (-np.arange(half, dtype=np.float32) / np.float32(half))
    pos = np.stack([p, P + p, PAST + p % NQ_S], 1).astype(np.float32)
    ang = (pos[:, :, None] * inv.astype(np.float32)).astype(np.float32)
    put("cos", np.cos(ang))
    put("sin", np.sin(ang))
    put("iota_slot", np.broadcast_to(np.arange(BT) + 1, (P, BT)))
    put("iota_e", np.broadcast_to(np.arange(NE), (P, NE)))
    put("e_base", np.broadcast_to(np.arange(NE) * BT + 1, (P, NE)))
    put("kmod", np.broadcast_to((p % NE)[:, None], (P, BT)))
    put("iota_ov", np.broadcast_to(np.arange(NOV), (P, NOV)))
    put("valid", np.stack([np.ones(P), np.ones(P), p < NS], 1))
    return np.ascontiguousarray(np.concatenate(cols, 1)), at


CONST_AT = constants()[1]
NCONST = sum(n for _, n in CONST_AT.values())


def build(nc, d):
    es = ExitStack()
    with es:
        def sb(name, cols, dt=F32):
            return es.enter_context(nc.sbuf_tensor(name, [P, cols], dt))[:, :]

        def sem(name):
            return es.enter_context(nc.semaphore(name))

        SLOT = 2048
        ring = sb("ring", 12 * SLOT)
        cst = sb("cst", NCONST)
        x_tok = sb("x_tok", 3 * D)
        h_tok = sb("h_tok", 3 * D)
        hT = sb("hT", KC * TT)
        kv_tok = sb("kv_tok", 3 * 768)
        mkv_tok = sb("mkv_tok", 2 * 512)
        cring = sb("cring", 2 * 2432)
        qT = sb("qT", 12 * TT)
        kT = sb("kT", 3 * TT)
        mkT = sb("mkT", 2 * LM)
        probs = sb("probs", 2 * 1024)
        pT = sb("pT", 2 * 512)
        w_rt = sb("w_rt", KC * NE)
        stat = sb("stat", 256)
        gains = sb("gains", 3 * KC)
        small = sb("small", 8 + 2 + NE)

        def const(name, n=P):
            a, w = CONST_AT[name]
            return cst[0:n, a:a + w]

        ident = const("ident")
        wblk = [ring[:, i * 2 * SLOT:(i + 1) * 2 * SLOT].rearrange("p (k n) -> p k n", n=512) for i in (0, 1)]
        aux = ring[:, 4 * SLOT:8 * SLOT]
        kTs = aux[:, 0:2432]
        s_probs = aux[:, 2432:4256]
        qw = aux[:, 4256:7136].rearrange("p (u r c n) -> p u r c n", u=2, r=2, c=12)
        qn = aux[:, 7136:7904].rearrange("p (r c n) -> p r c n", r=2, c=12)
        gate_area = ring[:, 8 * SLOT:12 * SLOT]
        gT = gate_area[:, 0:24 * TT].rearrange("p (m t) -> p m t", t=TT)
        mem_tok = gate_area[:, 0:2 * D].rearrange("p (t n) -> p t n", n=D)
        memT = gate_area[:, 2 * D:4 * D].rearrange("p (k t) -> p k t", t=2 * P)
        s_sum = [aux[0:NS, i * 512:(i + 1) * 512] for i in (0, 1)]
        q_tok = cring[:, 0:3 * 1536].rearrange("p (t n) -> p t n", n=1536)
        cslot = [cring[:, i * 2432:(i + 1) * 2432] for i in (0, 1)]
        x_v = x_tok.rearrange("p (t n) -> p t n", n=D)
        h_v = h_tok.rearrange("p (t n) -> p t n", n=D)
        oT = h_tok[:, 0:8 * TT].rearrange("p (k t) -> p k t", t=TT)
        hT_v = hT.rearrange("p (k t) -> p k t", t=TT)
        kv = kv_tok.rearrange("p (t n) -> p t n", n=768)
        mkv = mkv_tok.rearrange("p (t n) -> p t n", n=512)
        qT_v = qT.rearrange("p (c t) -> p c t", t=TT)
        kT_v = kT.rearrange("p (c t) -> p c t", t=TT)
        mkT_v = mkT.rearrange("p (c t) -> p c t", t=LM)
        pT_s = probs[:, 0:11 * P].rearrange("p (c q) -> p c q", q=P)
        pT_n = probs[0:NS, 11 * P:14 * P].rearrange("p (c q) -> p c q", q=P)
        wrt_v = w_rt.rearrange("p (k e) -> p k e", e=NE)
        gain_v = gains.rearrange("p (g k) -> p g k", k=KC)
        sink_p = small[:, 0:8]
        sink_s = small[:, 8:10]
        b_rt = small[:, 10:10 + NE]
        bias_raw = qT[0:NE, 0:3072]
        bias3 = kv_tok[:, 0:1536].bitcast(BF16)
        rt = qT
        sel = cring[:, 0:192].rearrange("p (t s) -> p t s", s=BT)
        g_min, g_sig, u_clip, act = [cring[:, 192 + 512 * n:704 + 512 * n] for n in range(4)]
        xTe = cring[:, 2240:2752].rearrange("p (k s) -> p k s", s=BT)
        aTe = cring[:, 2752:3264].rearrange("p (q m) -> p q m", m=P)
        y_sb = cring[:, 3264:3776]
        sel_b = cring[0:96, 3776:3808].bitcast(BF16)
        bsel = [cring[:, 3808 + 32 * n:3840 + 32 * n] for n in range(4)]
        ecols = cring[:, 3936:3944]
        sel_d = cring[:, 3944:4040]

        ps = es.enter_context(nc.psum_tensor("ps", [P, 8 * 512], F32))

        def bank(i, n=1):
            return ps[:, i * 512:(i + n) * 512]

        y_dram = nc.dram_tensor("expert_rows", (NBLK * BT, D), F32, kind="Internal").ap()

        names = """x_in mem_in cst_in small_in tail_self wblk0_in wblk1_in kc0_in kc1_in
        out_dma copy_dma v_self zeros sumsq root rstd ssum_ready hn_done tr_done tr_evicted proj_done
        proj_evicted rope_done gate_done gate_evicted gates_ready
        scores_done stat_ready exp_done p_ready pt_done pt_evicted pv_done o_evicted
        qw_ready kt_done ktv_evicted kta_evicted s_scores_b s_scores_done s_stat s_exp s_p_ready s_pt_done s_pt_evicted
        s_pv_done s_o_evicted br_done merged wout_done x2_done rt_done rt_evicted rank_lhs rank_done
        nov_done ov_done tables bias_raw_in
        sel_ready gath_done xt_ready gu_done g_ready sig_ready act_ready at_done at_evicted
        y_done y_evicted y_stored slices_used selb_ready
        gain_in rows_ready gath0_in gath1_in gath2_in comb fin_done""".split()
        S = {n: sem(n) for n in names}
        slice_in = [sem(f"slice{k}_in") for k in range(12)]
        block = es.enter_context(nc.Block())

        W_QKV, W_MEM, W_GATE, W_BR, W_OUT = range(5), 5, range(6, 12), (12, 13), (14, 15)
        wblk_dmas = [4 if i in W_BR else 1 for i in range(16)]

        def wblk_ready(eng, i):
            eng.wait_ge(S[f"wblk{i % 2}_in"], 16 * sum(wblk_dmas[i % 2:i + 1:2]))

        def wait_wblk_used(eng, i):
            if i <= W_MEM:
                eng.wait_ge(S["proj_done"], min(3 * i + 3, 17))
            elif i in W_GATE:
                eng.wait_ge(S["gate_done"], 4 * (i - 5))
            elif i in W_BR:
                eng.wait_ge(S["br_done"], 4 * (i - 11))
            else:
                eng.wait_ge(S["wout_done"], 3 * (i - 13))

        qkv_cols = [(0, 512), (512, 1024), (1024, 1536), (1536, 2048), (2048, 2304)]

        units = [(t, "a", h) for t in (0, 1) for h in (0, 1)] + \
                [(t, "b", h) for t in (0, 1) for h in range(4)] + [(t, "c", 0) for t in (0, 1)]
        NU = len(units)
        C_HEADS = (0, 2, 1, 3)

        def unit_shape(u):
            t, br, _ = units[u]
            nk = 2 * P if br == "c" or t == 1 else P
            return (3 if br == "b" else 4), nk

        def unit_probs(u):
            n, nk = unit_shape(u)
            return probs[:, (u % 2) * 1024:(u % 2) * 1024 + n * nk].rearrange("p (n k) -> p n k", k=nk)

        def unit_psum(u):
            n, nk = unit_shape(u)
            return bank(2 * (u % 2), 2)[:, 0:n * nk].rearrange("p (n k) -> p n k", k=nk)

        def st(u, kind, n=4):
            return stat[:, 12 * u + 4 * kind:12 * u + 4 * kind + n]

        norm_st = stat[:, 180:204]
        s_st = stat[:, 204:256]

        def head_pair(src, t, pair):
            return src[0:NTOK[t], t, pair * P:(pair + 1) * P]

        tr_groups = []
        for t in range(3):
            for c in (0, 4):
                tr_groups.append(([h_v[0:NTOK[t], t, (c + j) * P:(c + j + 1) * P] for j in range(4)],
                                  hT_v[:, c:c + 4, TOK0[t]:TOK0[t] + NTOK[t]], gain_v[:, 0, c:c + 4]))
        for t in range(2):
            for c in (0, 4):
                tr_groups.append(([mem_tok[:, t, (c + j) * P:(c + j + 1) * P] for j in range(4)],
                                  memT[:, c:c + 4, t * P:(t + 1) * P], gain_v[:, 1, c:c + 4]))
        TR_H, TR_Q = 10, 13
        for t in range(3):
            pairs = [head_pair(q_tok, t, n) for n in range(12)]
            for c in (0, 4, 8):
                tr_groups.append((pairs[c:c + 4], qT_v[:, c:c + 4, TOK0[t]:TOK0[t] + NTOK[t]], None))
            tr_groups.append(([head_pair(kv, t, n) for n in range(3)],
                              kT_v[:, 0:3, TOK0[t]:TOK0[t] + NTOK[t]], None))
        tr_groups.append(([mkv[:, t, m * P:(m + 1) * P] for m in range(2) for t in range(2)],
                          mkT_v[:, :, :].rearrange("p c (t n) -> p (c t) n", t=2), None))
        assert len(tr_groups) == TR_H + TR_Q

        def tr_bank(g):
            return bank(6 + g % 2) if g < TR_H else bank(g % 2)

        def tr_view(g):
            pieces, dst, _ = tr_groups[g]
            n = pieces[0].shape[0]
            return tr_bank(g)[:, 0:len(pieces) * n].rearrange("p (c n) -> p c n", n=n)

        def cache_b(s):
            return s[:, 0:NKR * 256].rearrange("p (r n) -> p r n", n=256)

        def cache_a(s):
            return s[:, 1792:1920]

        def cache_c(s):
            return s[:, 1920:2432].rearrange("p (r n) -> p r n", n=256)

        def kt_group(s, gi):
            cb, cc = cache_b(s), cache_c(s)
            return [
                ([cb[:, r, 0:P] for r in range(4)], 0),
                ([cb[:, r, P:2 * P] for r in range(4)], 1024),
                ([cb[:, r, 0:P] for r in range(4, 7)] + [cache_a(s)], 512),
                ([cb[:, r, P:2 * P] for r in range(4, 7)], 1536),
                ([cc[:, r, m * P:(m + 1) * P] for m in range(2) for r in range(2)], 1920),
            ][gi]

        SP = bank(0, 4)
        SC_B = SP[:, 0:NSM_B]
        SC_C = SP[:, NSM_B:NSM_B + LM]
        SC_A = SP[:, 1536:1536 + 2 * NSM_A].rearrange("p (v n) -> p v n", n=NSM_A)
        PR_B = s_probs[:, 0:NSM_B]
        PR_C = s_probs[:, NSM_B:NSM_B + LM]
        PR_A = s_probs[:, NSM_B + LM:NSM_B + LM + 2 * NSM_A].rearrange("p (v n) -> p v n", n=NSM_A)

        SO = bank(6)
        SO_A = SO[:, 0:256].rearrange("p (v j t) -> p v j t", v=2, j=4)
        SO_B = SO[:, 256:384].rearrange("p (m r t) -> p m r t", m=2, r=2)
        SO_C = SO[:, 384:512].rearrange("p (m r t) -> p m r t", m=2, r=2)

        def area(a, *shape):
            n = int(np.prod(shape))
            v = rt[:, a:a + n]
            if len(shape) == 2:
                return v.rearrange("p (a b) -> p a b", b=shape[1])
            if len(shape) == 3:
                return v.rearrange("p (a b c) -> p a b c", b=shape[1], c=shape[2])
            return v

        r_lg = area(0, 3, NE)
        r_mx = area(96, 3, 8)
        r_ix = area(120, 3, 8).bitcast(U32)
        r_ixf = area(144, 3, 8)
        r_d4 = area(168, 3, 4)
        r_gate = area(180, 3, 4)
        r_sum = area(192, 3)
        r_oh = area(200, 12, NE)
        r_tmp = area(584, 12, NE)
        r_mask = area(968, 3, NE)
        r_g1 = area(1064, 3, NE)
        r_rank = area(1160, 3, NE)
        r_ge = area(1256, 3, NE)
        r_novT = area(1352, P)
        r_ovs = area(1480, NE)
        r_ove = area(1512, NE)
        r_base = area(1544, NE)
        r_cmp = area(1576, NOV, NE)
        r_exp = area(2152, NOV)
        r_tab = area(2170, NOV + 1).bitcast(I32)
        r_idxf = area(2190, 12)
        r_idx = area(2202, 12).bitcast(U32)
        r_cnt = area(2214, 4)
        r_tot = area(2220, 1)
        g_final = area(2400, D)

        SMALL_IN = 16 * 14
        KV_OUT = 16 * 10
        GATES_FIRST = 4
        GATES_AFTER_BATCH = (0, 2, 4, 6)

        def evict_kt(eng, b, gi, copy, done):
            g = 5 * b + gi
            eng.wait_ge(S["kt_done"], g + 1)
            if b >= 1:
                eng.wait_ge(S["s_scores_b"], b)
            pieces, at = kt_group(cslot[b % 2], gi)
            n = len(pieces) * P
            copy(kTs[:, at:at + n], bank(4 + g % 2)[:, 0:n]).then_inc(S[done], 1)

        @block.sync
        def _(sp):
            sp.dma_start(x_v[:, 0:2, :], d["x_prompt"][0].rearrange("(t p) n -> p t n", p=P)).then_inc(S["x_in"], 16)
            sp.dma_start(x_v[0:NS, 2, :], d["x_sample"].rearrange("b i n -> (b i) n")).then_inc(S["x_in"], 16)
            sp.dma_start(cst, d["consts"]).then_inc(S["cst_in"], 16)
            w_in = d["w_in"][0].rearrange("(k p) n -> p k n", p=P)
            w_out = d["w_out"][0].rearrange("(k p) n -> p k n", p=P)

            def load_wblk(i):
                dst, s = wblk[i % 2], S[f"wblk{i % 2}_in"]
                if i >= 2:
                    wait_wblk_used(sp, i - 2)
                if i in W_QKV:
                    a, b = qkv_cols[i]
                    sp.dma_start(dst[:, :, 0:b - a], w_in[:, :, a:b]).then_inc(s, 16)
                elif i == W_MEM:
                    sp.dma_start(dst, d["w_mem_kv"][0].rearrange("(k p) n -> p k n", p=P)).then_inc(s, 16)
                elif i in W_GATE:
                    a = GATE0 + 512 * (i - 6)
                    sp.dma_start(dst, w_in[:, :, a:a + 512]).then_inc(s, 16)
                elif i in W_BR:
                    n = slice(512 * (i - 12), 512 * (i - 11))
                    a = d["w_br_a"][0].rearrange("(v j q) n -> v q j n", v=2, q=HD)
                    sp.dma_start(dst[0:64, 0:4, :], a[0][:, :, n]).then_inc(s, 16)
                    sp.dma_start(dst[64:128, 0:4, :], a[1][:, :, n]).then_inc(s, 16)
                    sp.dma_start(dst[:, 4:6, :], d["w_br_b"][0].rearrange("(m p) n -> p m n", p=P)[:, :, n]).then_inc(s, 16)
                    sp.dma_start(dst[:, 6:8, :], d["w_br_c"][0].rearrange("(m p) n -> p m n", p=P)[:, :, n]).then_inc(s, 16)
                else:
                    n = slice(512 * (i - 14), 512 * (i - 13))
                    sp.dma_start(dst, w_out[:, :, n]).then_inc(s, 16)

            copies = [(x, b) for x in ("k", "v") for b in range(NB_S)]

            COPY_AFTER = (2, 3, 4, 5)
            def copy_cache():
                if copies:
                    x, b = copies.pop(0)
                    n = (LB - NQ_S) * 256
                    src = d[f"cache_dil_{x}"][0, b].rearrange("r h n -> (r h n)")[NQ_S * 256:]
                    dst = d[f"dil_{x}_s"][0, b].rearrange("r h n -> (r h n)")[0:n]
                    sp.dma_start(dst.rearrange("(a n) -> a n", a=64), src.rearrange("(a n) -> a n", a=64)) \
                        .then_inc(S["copy_dma"], 16)

            def load_cache(i):
                x, b = "kv"[i // NB_S], i % NB_S
                s, sm = cslot[i % 2], S[f"kc{i % 2}_in"]
                if 2 <= i < NB_S + 2:
                    sp.wait_ge(S["kt_done"], 5 * (i - 1))
                elif i >= NB_S + 2:
                    sp.wait_ge(S["s_pv_done"], i - 1 - NB_S)
                src = d[f"cache_dil_{x}"][0, b].rearrange("r h n -> r (h n)")
                cb = cache_b(s)
                sp.dma_start(cb[:, 0:4, :], src[1536:2048].rearrange("(r p) n -> p r n", p=P)).then_inc(sm, 16)
                far = src[0:1536].rearrange("(r q s) n -> r q s n", r=3, s=16)
                for r in range(3):
                    sp.dma_start(cb[:, 4 + r, :], far[r, :, 0:4, :]).then_inc(sm, 16)
                sp.dma_start(cache_a(s), d[f"cache_swa_{x}"][0, b].rearrange("r h n -> r (h n)")).then_inc(sm, 16)
                sp.dma_start(cache_c(s), d[f"cache_mem_{x}"][0, b].rearrange("(r p) h n -> p r (h n)", p=P)).then_inc(sm, 16)

            for i in range(9):
                load_wblk(i)
                if i >= 4:
                    copy_cache()
            sp.wait_ge(S["tr_evicted"], TR_H + TR_Q)
            load_cache(0)
            load_cache(1)
            for i in (9, 10, 11):
                load_wblk(i)
                copy_cache()
            for x in "kv":
                n = (LA - NQ_S) * 128
                src = d[f"cache_swa_{x}"][0].rearrange("b r h n -> b (r h n)")[:, NQ_S * 128:]
                dst = d[f"swa_{x}_s"][0].rearrange("b r h n -> b (r h n)")[:, 0:n]
                sp.dma_start(dst.rearrange("b (a n) -> b a n", a=16), src.rearrange("b (a n) -> b a n", a=16)) \
                    .then_inc(S["copy_dma"], 16)

            for i in range(2, 6):
                load_cache(i)
                if i in COPY_AFTER:
                    copy_cache()
            load_wblk(12)
            for i in range(6, 10):
                load_cache(i)
                if i in COPY_AFTER:
                    copy_cache()
            load_wblk(13)
            for i in range(10, 16):
                load_cache(i)
                if i in COPY_AFTER:
                    copy_cache()
            def load_slice(k, e):
                dst = ring[:, k * SLOT:(k + 1) * SLOT]
                if k < 8:
                    src = d["w_gate_up"][0, e, k * P:(k + 1) * P, :]
                else:
                    src = d["w_down"][0, e, (k - 8) * 2 * P:(k - 7) * 2 * P, :].rearrange("(c p) n -> p c n", p=P)
                    dst = dst.rearrange("p (c n) -> p c n", c=2)
                return sp.dma_start(dst, src)

            sp.wait_ge(S["s_pt_done"], 4)
            for k in range(4, 8):
                load_slice(k, 0).then_inc(slice_in[k], 16)
            load_wblk(14)
            load_wblk(15)
            sp.wait_ge(S["merged"], 8)
            for k in range(8, 12):
                load_slice(k, 0).then_inc(slice_in[k], 16)
            wait_wblk_used(sp, 15)
            for k in range(0, 4):
                load_slice(k, 0).then_inc(slice_in[k], 16)
            while copies:
                copy_cache()

            def load_dyn(k, e):
                dst = ring[:, k * SLOT:(k + 1) * SLOT]
                if k < 8:
                    src = d["w_gate_up"][0][bass.ds(e, 1), k * P:(k + 1) * P, :].rearrange("o p n -> (o p) n")
                else:
                    src = d["w_down"][0][bass.ds(e, 1), (k - 8) * 2 * P:(k - 7) * 2 * P, :] \
                        .rearrange("o (c p) n -> (o p) c n", p=P)
                    dst = dst.rearrange("p (c n) -> p c n", c=2)
                return sp.dma_start(dst, src)

            def slice_free(k, b):
                if k < 11:
                    sp.wait_ge(S["slices_used"], 11 * b + (k - 10))
                else:
                    sp.wait_ge(S["y_done"], b)

            with sp.Fori(1, NE) as b:
                for k in range(12):
                    slice_free(k, b)
                    load_dyn(k, b).then_inc(slice_in[k], 16)
            sp.wait_ge(S["tables"], 1)
            n_blk = sp.value_load(r_tab[0:1, NOV:NOV + 1], min_val=NE, max_val=NBLK)
            with sp.Fori(NE, NBLK) as b:
                with sp.If(b < n_blk):
                    e = sp.value_load(r_tab[0:1, bass.ds(b - NE, 1)], min_val=0, max_val=NE - 1)
                    for k in range(12):
                        slice_free(k, b)
                        load_dyn(k, e).then_inc(slice_in[k], 16)
            sp.wait_ge(S["copy_dma"], 16 * (2 * NB_S + 2))

        @block.gpsimd
        def _(pool):
            pool.dma_start(mem_tok, d["mem_prompt"][0].rearrange("(t p) n -> p t n", p=P)).then_inc(S["mem_in"], 16)
            n_small = 0
            for dst, src in [(gain_v[:, 0, :], d["norm_attn"][0].rearrange("(k p) -> p k", p=P)),
                             (gain_v[:, 1, :], d["norm_mem"][0].rearrange("(k p) -> p k", p=P)),
                             (gain_v[:, 2, :], d["norm_ffn"][0].rearrange("(k p) -> p k", p=P)),
                             (sink_p, d["sinks"].to_broadcast([P, 8])),
                             (b_rt, d["b_router"].to_broadcast([P, NE]))]:
                pool.dma_start(dst, src, allow_slow_non_contiguous=True).then_inc(S["small_in"], 16)
                n_small += 1
            for j in range(4):
                for v in range(2):
                    pool.dma_start(sink_s[32 * j:32 * j + 32, v:v + 1],
                                   d["sinks"][:, 4 * v + j:4 * v + j + 1].to_broadcast([32, 1]),
                                   allow_slow_non_contiguous=True).then_inc(S["small_in"], 16)
                    n_small += 1
            pool.dma_start(wrt_v, d["w_router"][0].rearrange("(k p) e -> p k e", p=P)).then_inc(S["small_in"], 16)
            n_small += 1
            assert 16 * n_small == SMALL_IN
            pool.memset(aux[:, 4256:7904], 0.0).then_inc(S["zeros"], 1)
            pool.wait_ge(S["zeros"], 1)

            pool.wait_ge(S["tr_evicted"], TR_H + TR_Q)
            pool.wait_ge(S["y_stored"], 16)
            for r in range(2):
                h = slice(64 * r, 64 * r + 64)
                ins = pool.tensor_copy(qn[h, r, :, :], qT_v[h, :, SEQ:TT])
            ins.then_inc(S["qw_ready"], 1)
            for b in range(NB_S):
                if b >= 2:
                    pool.wait_ge(S["s_scores_b"], b - 1)
                for r in range(2):
                    h = slice(64 * r, 64 * r + 64)
                    ins = pool.tensor_copy(qw[h, b % 2, r, :, 28:32], qT_v[h, :, SEQ + 4 * b:SEQ + 4 * b + 4])
                ins.then_inc(S["qw_ready"], 1)
            pool.wait_ge(S["s_scores_done"], 1)
            pool.dma_start(bias_raw[:, 0:2048], d["b_gate_up"][0]).then_inc(S["bias_raw_in"], 16)
            pool.dma_start(bias_raw[:, 2048:3072], d["b_down"][0]).then_inc(S["bias_raw_in"], 16)
            pool.wait_ge(S["tables"], 1)
            n_blk = pool.value_load(r_tab[0:1, NOV:NOV + 1], min_val=NE, max_val=NBLK)
            pool.dma_start(g_final, d["norm_final"].unsqueeze(0).to_broadcast([P, D])).then_inc(S["gain_in"], 16)
            pool.wait_ge(S["y_stored"], 32 * n_blk + 16)
            pool.tensor_tensor(r_idxf, r_idxf, const("ones")[:, 0:3 * TOPK], ALU.subtract).then_inc(S["rows_ready"], 1)
            pool.wait_ge(S["rows_ready"], 1)
            pool.tensor_copy(r_idx, r_idxf).then_inc(S["rows_ready"], 1)
            pool.wait_ge(S["rows_ready"], 2)
            for j in range(3 * TOPK):
                t = j // TOPK
                n = NTOK[t]
                pool.indirect_dma_start(
                    out=ring[0:n, j * D:(j + 1) * D], out_offset=None, in_=y_dram[:, :],
                    in_offset=bass.IndirectOffsetOnAxis(ap=r_idx[0:n, j:j + 1], axis=0),
                ).then_inc(S[f"gath{t}_in"], 16)

        @block.scalar
        def _(act_e):
            def sumsq_and_scale(src, dst, n_rows, col, junk):
                act_e.activation(junk, src, ACT.Square, accum_out=norm_st[0:n_rows, col:col + 1]).then_inc(S["sumsq"], 1)

            tiles = [(x_v, h_v, t, NTOK[t]) for t in range(3)] + [(mem_tok, mem_tok, t, P) for t in range(2)]
            act_e.wait_ge(S["x_in"], 32)
            act_e.wait_ge(S["v_self"], 1)
            for n, (src, dst, t, rows) in enumerate(tiles):
                if n == 3:
                    act_e.wait_ge(S["mem_in"], 16)
                junk = h_v if n < 3 else memT.rearrange("p k t -> p (k t)").rearrange("p (t n) -> p t n", n=D)
                sumsq_and_scale(src[0:rows, t, :], None, rows, n, junk[0:rows, t, :])
            act_e.wait_ge(S["zeros"], 1)
            act_e.dma_start(y_dram[NE * BT:, :].rearrange("(r p) n -> p r n", p=P),
                            aux[:, 4256:4256 + D].unsqueeze(1).to_broadcast([P, NOV * BT // P, D])) \
                .then_inc(S["y_stored"], 16)
            act_e.wait_ge(S["rstd"], 1)
            act_e.wait_ge(S["sumsq"], 5)
            act_e.activation(norm_st[:, 8:13], norm_st[:, 8:13], ACT.Sqrt).then_inc(S["root"], 1)
            act_e.wait_ge(S["rstd"], 2)
            for n, (src, dst, t, rows) in enumerate(tiles):
                act_e.activation(dst[0:rows, t, :], src[0:rows, t, :], ACT.Copy,
                                 scale=norm_st[0:rows, 16 + n:17 + n]).then_inc(S["hn_done"], 1)

            for n in range(5):
                for t in range(3):
                    act_e.wait_ge(S["proj_done"], 3 * n + t + 1)
                    r = NTOK[t]
                    if t < 2:
                        pb = bank((n % 2) * 3 + t)
                    else:
                        act_e.wait_ge(S["ssum_ready"], n + 1)
                        pb = s_sum[n % 2]
                    q, kvt = q_tok[0:r, t, :], kv[0:r, t, :]
                    if n == 0:
                        ins = act_e.activation(q[:, 0:512].rearrange("p (j v n) -> p v j n", v=2, n=HD),
                                               pb.rearrange("p (v j n) -> p v j n", v=2, n=HD), ACT.Copy, scale=QSCALE)
                    elif n == 1:
                        act_e.activation(kvt[:, 0:128], pb[:, 0:128], ACT.Copy)
                        act_e.activation(kvt[:, 384:512], pb[:, 128:256], ACT.Copy)
                        ins = act_e.activation(q[:, 512:768], pb[:, 256:512], ACT.Copy, scale=QSCALE)
                    elif n == 2:
                        ins = act_e.activation(q[:, 768:1280], pb, ACT.Copy, scale=QSCALE)
                    elif n == 3:
                        act_e.activation(kvt[:, 128:384], pb[:, 0:256], ACT.Copy)
                        ins = act_e.activation(kvt[:, 512:768], pb[:, 256:512], ACT.Copy)
                    else:
                        ins = act_e.activation(q[:, 1280:1536], pb[:, 0:256], ACT.Copy, scale=QSCALE)
                    ins.then_inc(S["proj_evicted"], 1)
            for t in range(2):
                act_e.wait_ge(S["proj_done"], 16 + t)
                act_e.activation(mkv[:, t, :], bank(3 + t), ACT.Copy).then_inc(S["proj_evicted"], 1)

            act_e.wait_ge(S["proj_evicted"], 17)
            act_e.wait_ge(S["rope_done"], 6)
            outs = 0
            for x, (a, b) in (("k", (0, 128)), ("v", (384, 512))):
                act_e.dma_start(d[f"swa_{x}_p"][0, 0].rearrange("r h n -> r (h n)"), kv[:, 1, a:b]).then_inc(S["out_dma"], 16)
                act_e.dma_start(d[f"swa_{x}_s"][0].rearrange("b r h n -> b r (h n)")[:, LA - NQ_S:, :],
                                kv[0:NS, 2, a:b]).then_inc(S["out_dma"], 16)
                outs += 2
            for x, (a, b) in (("k", (128, 384)), ("v", (512, 768))):
                act_e.dma_start(d[f"dil_{x}_p"][0, 0].rearrange("(t p) h n -> p t (h n)", p=P), kv[:, 0:2, a:b]).then_inc(S["out_dma"], 16)
                act_e.dma_start(d[f"dil_{x}_s"][0].rearrange("b r h n -> b r (h n)")[:, LB - NQ_S:, :],
                                kv[0:NS, 2, a:b]).then_inc(S["out_dma"], 16)
                outs += 2
            for x, a in (("k", 0), ("v", 256)):
                act_e.dma_start(d[f"mem_{x}_p"][0, 0].rearrange("(t p) h n -> p t (h n)", p=P),
                                mkv[:, :, a:a + 256]).then_inc(S["out_dma"], 16)
                outs += 1
            assert 16 * outs == KV_OUT

            gate_n = [0]

            def evict_gate():
                m = gate_n[0]
                gate_n[0] += 1
                act_e.wait_ge(S["gate_done"], m + 1)
                act_e.activation(gT[:, m, :], bank(7)[:, 0:TT], ACT.Copy).then_inc(S["gate_evicted"], 1)

            def exps(u):
                t, br, h = units[u]
                n, nk = unit_shape(u)
                pr = unit_probs(u)
                act_e.wait_ge(S["stat_ready"], u + 1)
                if br == "b":
                    act_e.activation(pr.rearrange("p n k -> p (n k)"), pr.rearrange("p n k -> p (n k)"), ACT.Exp,
                                     bias=st(u, 0, 1), accum_out=st(u, 1, 1)).then_inc(S["exp_done"], 1)
                    return
                src = unit_psum(u) if br == "c" else pr
                for j in range(4):
                    ins = act_e.activation(pr[:, j, :], src[:, j, :], ACT.Exp, bias=st(u, 0)[:, j:j + 1],
                                           accum_out=st(u, 1)[:, j:j + 1])
                if br == "a":
                    ins = act_e.activation(st(u, 2), st(u, 2), ACT.Exp)
                ins.then_inc(S["exp_done"], 1)

            def pt_view(u):
                t, br, h = units[u]
                n, nk = unit_shape(u)
                m = 1 if br == "b" else 4
                return bank(4, 2).rearrange("p (c x) -> p c x", x=512)[:, 0:nk // P, 0:m * P], \
                    pT.rearrange("p (c x) -> p c x", x=512)[:, 0:nk // P, 0:m * P]

            def evict_pt(u):
                act_e.wait_ge(S["pt_done"], u + 1)
                if u >= 1:
                    act_e.wait_ge(S["pv_done"], u)
                src, dst = pt_view(u)
                act_e.activation(dst, src, ACT.Copy).then_inc(S["pt_evicted"], 1)

            def evict_o(u):
                t, br, h = units[u]
                act_e.wait_ge(S["pv_done"], u + 1)
                o = bank(6)
                tok = slice(TOK0[t], TOK0[t] + P)
                if br == "a":
                    r = slice(64 * h, 64 * h + 64)
                    ins = act_e.activation(oT[r, 0:4, tok], o[r, :].rearrange("p (j q) -> p j q", q=P), ACT.Copy)
                elif br == "b":
                    r = slice(64 * (h % 2), 64 * (h % 2) + 64)
                    ins = act_e.activation(oT[r, 4 + h // 2, tok], o[r, 0:P], ACT.Copy)
                else:
                    for par in range(2):
                        r = slice(64 * par, 64 * par + 64)
                        ins = act_e.activation(oT[r, 6:8, tok], o[r, 0:256].rearrange("p (m q) -> p m q", q=P), ACT.Copy)
                ins.then_inc(S["o_evicted"], 1)

            for _ in range(GATES_FIRST):
                evict_gate()
            exps(0)
            for u in range(NU):
                if u + 1 < NU:
                    exps(u + 1)
                evict_gate()
                evict_pt(u)
                evict_o(u)

            for b in range(NB_S):
                for gi in range(5):
                    g = 5 * b + gi
                    if g % 2 == 0:
                        continue
                    evict_kt(act_e, b, gi, lambda o, i: act_e.activation(o, i, ACT.Copy), "kta_evicted")
                if b in GATES_AFTER_BATCH:
                    evict_gate()
            evict_gate()
            evict_gate()
            act_e.wait_ge(S["s_stat"], 1)
            act_e.activation(PR_B, PR_B, ACT.Exp, bias=s_st[:, 0:1], accum_out=s_st[:, 4:5])
            for v in range(2):
                act_e.activation(PR_A[:, v, :], PR_A[:, v, :], ACT.Exp, bias=s_st[:, 2 + v:3 + v],
                                 accum_out=s_st[:, 6 + v:7 + v])
            act_e.activation(s_st[:, 8:10], s_st[:, 8:10], ACT.Exp)
            act_e.activation(PR_C, SC_C, ACT.Exp, bias=s_st[:, 1:2], accum_out=s_st[:, 5:6]).then_inc(S["s_exp"], 1)
            for g in range(4):
                act_e.wait_ge(S["s_pt_done"], g + 1)
                if g < 3:
                    n = 4 if g < 2 else 3
                    ins = act_e.activation(pT_s[:, 4 * g:4 * g + n, :],
                                           bank(4 + g % 2)[:, 0:n * P].rearrange("p (c q) -> p c q", q=P), ACT.Copy)
                else:
                    ins = act_e.activation(pT_n, bank(5)[0:NS, 0:3 * P].rearrange("p (c q) -> p c q", q=P), ACT.Copy)
                ins.then_inc(S["s_pt_evicted"], 1)
            act_e.wait_ge(S["gate_evicted"], 24)
            g3 = gT.rearrange("p (r m) t -> p m r t", r=3)
            for m in range(8):
                act_e.activation(g3[:, m], g3[:, m], ACT.Sigmoid).then_inc(S["gates_ready"], 1)

            for t in range(3):
                act_e.wait_ge(S["x2_done"], t + 1)
                if t == 0:
                    act_e.wait_ge(S["merged"], 8)
                    act_e.wait_ge(S["br_done"], 8)
                sumsq_and_scale(x_v[0:NTOK[t], t, :], None, NTOK[t], t, h_v[0:NTOK[t], t, :])
            act_e.wait_ge(S["rstd"], 3)
            act_e.wait_ge(S["sumsq"], 8)
            act_e.activation(norm_st[:, 8:11], norm_st[:, 8:11], ACT.Sqrt).then_inc(S["root"], 1)
            act_e.wait_ge(S["rstd"], 4)
            for t in range(3):
                act_e.activation(h_v[0:NTOK[t], t, :], x_v[0:NTOK[t], t, :], ACT.Copy,
                                 scale=norm_st[0:NTOK[t], 16 + t:17 + t]).then_inc(S["hn_done"], 1)
            act_e.wait_ge(S["rank_lhs"], 1)
            act_e.activation(r_d4, r_d4, ACT.Exp).then_inc(S["nov_done"], 1)
            act_e.wait_ge(S["nov_done"], 1)

            def act_block(b):
                act_e.wait_ge(S["g_ready"], b + 1)
                act_e.activation(g_sig, g_min, ACT.Sigmoid, scale=ALPHA).then_inc(S["sig_ready"], 1)
                act_e.wait_ge(S["at_done"], b + 1)
                act_e.activation(aTe, bank(4)[:, :].rearrange("p (q m) -> p q m", m=P), ACT.Copy) \
                    .then_inc(S["at_evicted"], 1)
                act_e.wait_ge(S["y_done"], b + 1)
                act_e.wait_ge(S["y_stored"], 32 * b + 16)
                act_e.activation(y_sb, bank(5), ACT.Copy).then_inc(S["y_evicted"], 1)
                act_e.wait_ge(S["y_evicted"], b + 1)
                for h in range(2):
                    act_e.dma_start(y_dram[bass.ds(b * BT, BT), h * 512:(h + 1) * 512],
                                    y_sb[64 * h:64 * h + 64, :]).then_inc(S["y_stored"], 16)

            with act_e.Fori(0, NE) as b:
                act_block(b)
            act_e.wait_ge(S["tables"], 1)
            n_blk = act_e.value_load(r_tab[0:1, NOV:NOV + 1], min_val=NE, max_val=NBLK)
            with act_e.Fori(NE, NBLK) as b:
                with act_e.If(b < n_blk):
                    act_block(b)

            for t in range(3):
                act_e.wait_ge(S["comb"], 4 * t + 4)
                r = NTOK[t]
                sumsq_and_scale(x_v[0:r, t, :], None, r, t, ring[0:r, (4 * t) * D:(4 * t + 1) * D])
            act_e.wait_ge(S["rstd"], 5)
            act_e.wait_ge(S["sumsq"], 11)
            act_e.activation(norm_st[:, 8:11], norm_st[:, 8:11], ACT.Sqrt).then_inc(S["root"], 1)
            act_e.wait_ge(S["fin_done"], 2)
            act_e.dma_start(d["y_p"][0].rearrange("(t p) n -> p t n", p=P), x_v[:, 0:2, :]).then_inc(S["out_dma"], 16)
            act_e.wait_ge(S["fin_done"], 3)
            act_e.dma_start(d["y_s"].rearrange("b i n -> (b i) n"), x_v[0:NS, 2, :]).then_inc(S["out_dma"], 16)
            act_e.wait_ge(S["out_dma"], KV_OUT + 32)

        @block.tensor
        def _(pe):
            def transposes(g):
                pieces, _, _ = tr_groups[g]
                v = tr_view(g)
                for j, src in enumerate(pieces):
                    n = src.shape[0]
                    ins = pe.transpose(v[:, j, :], src, ident[0:n, 0:n])
                ins.then_inc(S["tr_done"], 1)

            def k_rows(t, k):
                return slice(0, P) if t < 2 else slice(NS * (k % 4), NS * (k % 4) + NS)

            def k_group(t, k):
                if t < 2:
                    return dict(start=(k == 0), stop=(k == KC - 1))
                return dict(start=(k < 4), stop=(k >= KC - 4))

            pe.wait_ge(S["cst_in"], 16)
            for g in range(TR_H):
                pe.wait_ge(S["hn_done"], g // 2 + 1)
                if g >= 2:
                    pe.wait_ge(S["tr_evicted"], g - 1)
                transposes(g)

            for n in range(5):
                wblk_ready(pe, n)
                pe.wait_ge(S["tr_evicted"], 6)
                a, b = qkv_cols[n]
                for t in range(3):
                    if n >= 2:
                        pe.wait_ge(S["proj_evicted"], 3 * (n - 2) + t + 1)
                    for k in range(KC):
                        ins = pe.matmul(bank((n % 2) * 3 + t)[k_rows(t, k), 0:b - a],
                                        hT_v[:, k, TOK0[t]:TOK0[t] + NTOK[t]], wblk[n % 2][:, k, 0:b - a],
                                        **k_group(t, k))
                    ins.then_inc(S["proj_done"], 1)
            wblk_ready(pe, W_MEM)
            pe.wait_ge(S["tr_evicted"], TR_H)
            for t in range(2):
                pe.wait_ge(S["proj_evicted"], 10 + t)
                for k in range(KC):
                    ins = pe.matmul(bank(3 + t), memT[:, k, t * P:(t + 1) * P], wblk[1][:, k, :],
                                    start=(k == 0), stop=(k == KC - 1))
                ins.then_inc(S["proj_done"], 1)

            gate_n = [0]

            def gate_tile():
                m = gate_n[0]
                gate_n[0] += 1
                blk = 6 + m // 4
                if m % 4 == 0:
                    wblk_ready(pe, blk)
                if m >= 1:
                    pe.wait_ge(S["gate_evicted"], m)
                for k in range(KC):
                    ins = pe.matmul(bank(7)[:, 0:TT], wblk[blk % 2][:, k, (m % 4) * P:(m % 4 + 1) * P],
                                    hT_v[:, k, :], start=(k == 0), stop=(k == KC - 1))
                ins.then_inc(S["gate_done"], 1)

            for _ in range(GATES_FIRST):
                gate_tile()

            for n in range(TR_Q):
                g = TR_H + n
                if n < 12:
                    pe.wait_ge(S["rope_done"], 2 * (n // 4) + 2)
                else:
                    pe.wait_ge(S["proj_evicted"], 17)
                if n >= 2:
                    pe.wait_ge(S["tr_evicted"], g - 1)
                transposes(g)

            def scores(u):
                t, br, h = units[u]
                n, nk = unit_shape(u)
                out = unit_psum(u)
                tok = slice(TOK0[t], TOK0[t] + P)
                k0 = 0
                if u >= 2:
                    pe.wait_ge(S["exp_done"], u - 1)
                for j in range(n):
                    if br == "a":
                        r, chunk, keys = h, j, kT_v[64 * h:64 * h + 64, 0, k0:k0 + nk]
                    elif br == "b":
                        r, chunk = h % 2, 4 + 2 * j + h // 2
                        keys = kT_v[64 * r:64 * r + 64, 1 + h // 2, k0:k0 + nk]
                    else:
                        hh = C_HEADS[j]
                        r, chunk = hh % 2, 10 + hh // 2
                        keys = mkT_v[64 * r:64 * r + 64, hh // 2, :]
                    ins = pe.matmul(out[:, j, :], qT_v[64 * r:64 * r + 64, chunk, tok], keys, start=True, stop=True)
                ins.then_inc(S["scores_done"], 1)

            def p_transposes(u):
                t, br, h = units[u]
                n, nk = unit_shape(u)
                pr = unit_probs(u)
                pe.wait_ge(S["p_ready"], u + 1)
                if u >= 1:
                    pe.wait_ge(S["pt_evicted"], u)
                for c in range(nk // P):
                    for j in range(1 if br == "b" else 4):
                        ins = pe.transpose(bank(4 + c)[:, j * P:(j + 1) * P], pr[:, j, c * P:(c + 1) * P], ident)
                ins.then_inc(S["pt_done"], 1)

            def values(u):
                t, br, h = units[u]
                n, nk = unit_shape(u)
                pe.wait_ge(S["pt_evicted"], u + 1)
                if u >= 1:
                    pe.wait_ge(S["o_evicted"], u)
                pv = pT.rearrange("p (c x) -> p c x", x=512)
                nc_ = nk // P
                if br == "c":
                    for j, hh in enumerate(C_HEADS):
                        r = 64 * (hh % 2)
                        for c in range(nc_):
                            ins = pe.matmul(bank(6)[r:r + 64, (hh // 2) * P:(hh // 2 + 1) * P],
                                            mkv[:, c, 256 + hh * 64:320 + hh * 64], pv[:, c, j * P:(j + 1) * P],
                                            start=(c == 0), stop=(c == nc_ - 1))
                else:
                    r = 64 * h if br == "a" else 64 * (h % 2)
                    v0 = (384 if br == "a" else 512) + 64 * h
                    m = 512 if br == "a" else P
                    for c in range(nc_):
                        ins = pe.matmul(bank(6)[r:r + 64, 0:m], kv[:, c, v0:v0 + 64], pv[:, c, 0:m],
                                        start=(c == 0), stop=(c == nc_ - 1))
                ins.then_inc(S["pv_done"], 1)

            pe.wait_ge(S["tr_evicted"], TR_H + TR_Q)
            scores(0)
            scores(1)
            for u in range(NU):
                gate_tile()
                p_transposes(u)
                if u + 2 < NU:
                    scores(u + 2)
                values(u)

            pe.wait_ge(S["o_evicted"], NU)
            pe.wait_ge(S["exp_done"], NU)
            for b in range(NB_S):
                pe.wait_ge(S[f"kc{b % 2}_in"], 96 * (b // 2 + 1))
                for gi in range(5):
                    g = 5 * b + gi
                    if g >= 2:
                        pe.wait_ge(S["ktv_evicted" if g % 2 == 0 else "kta_evicted"], (g - 2) // 2 + 1)
                    pieces, _ = kt_group(cslot[b % 2], gi)
                    for j, src in enumerate(pieces):
                        ins = pe.transpose(bank(4 + g % 2)[:, j * P:(j + 1) * P], src, ident)
                    ins.then_inc(S["kt_done"], 1)
                if b in GATES_AFTER_BATCH:
                    gate_tile()
                done = 5 * (b + 1)
                pe.wait_ge(S["ktv_evicted"], (done + 1) // 2)
                pe.wait_ge(S["kta_evicted"], done // 2)
                pe.wait_ge(S["qw_ready"], b + 2)
                win = slice(28 - 4 * b, 60 - 4 * b)
                first, last = b == 0, b == NB_S - 1

                def add(out, lhs, rhs, start):
                    return pe.matmul(out, lhs, rhs, start=start, stop=last, skip_group_check=True)

                for part in range(5):
                    for h in range(4):
                        m, r = h // 2, h % 2
                        row = slice(32 * h, 32 * h + 32)
                        kb = kTs[:, m * 1024:m * 1024 + 896]
                        q = qw[:, b % 2, r]
                        if part == 0:
                            add(SP[row, 0:512], q[:, 6 + m, win], kb[:, 0:512], first)
                        elif part == 1:
                            add(SP[row, 512:896], q[:, 8 + m, win], kb[:, 512:896], first)
                        elif part == 2:
                            add(SP[row, 896:1024], q[:, 8 + m, win],
                                kb[:, 0:512].rearrange("p (a s) -> p a s", s=16)[:, :, 0:4], False)
                        elif part == 3:
                            add(SP[row, 1024:1152], q[:, 4 + m, win], kb[:, 384:512], first)
                        else:
                            add(SP[row, NSM_B:NSM_B + LM], q[:, 10 + m, win],
                                kTs[:, 1920 + m * LM:1920 + (m + 1) * LM], False)
                for v in range(2):
                    for j in range(4):
                        ins = add(SC_A[32 * j:32 * j + 32, v, 0:LA], qw[:, b % 2, v, j, win], kTs[:, 896:1024],
                                  first and v == 0)
                ins.then_inc(S["s_scores_b"], 1)
            for g in range(3):
                for h in range(4):
                    m, r = h // 2, h % 2
                    pe.matmul(SP[32 * h:32 * h + 32, 1152 + NS * g:1152 + NS * (g + 1)], qn[:, r, 4 + 2 * g + m, :],
                              kT_v[:, 1 + m, SEQ:TT], start=False, stop=True, skip_group_check=True)
            for v in range(2):
                for j in range(4):
                    ins = pe.matmul(SC_A[32 * j:32 * j + 32, v, LA:NSM_A], qn[:, v, j, :], kT_v[:, 0, SEQ:TT],
                                    start=False, stop=True, skip_group_check=True)
            ins.then_inc(S["s_scores_done"], 1)

            gate_tile()
            gate_tile()
            pe.wait_ge(S["s_p_ready"], 1)
            srcs = [PR_B[:, c * P:(c + 1) * P] for c in range(7)] + [PR_A[:, v, 0:P] for v in range(2)] + \
                   [PR_C[:, c * P:(c + 1) * P] for c in range(2)]
            for g in range(3):
                if g == 2:
                    pe.wait_ge(S["s_pt_evicted"], 1)
                for j, src in enumerate(srcs[4 * g:4 * g + 4]):
                    ins = pe.transpose(bank(4 + g % 2)[:, j * P:(j + 1) * P], src, ident)
                ins.then_inc(S["s_pt_done"], 1)
            pe.wait_ge(S["s_pt_evicted"], 2)
            for j, src in enumerate([PR_B[:, 1152:1152 + NS], PR_A[:, 0, LA:], PR_A[:, 1, LA:]]):
                ins = pe.transpose(bank(5)[0:NS, j * P:(j + 1) * P], src, ident)
            ins.then_inc(S["s_pt_done"], 1)

            pe.wait_ge(S["s_pt_evicted"], 4)
            acc = dict(start=False, skip_group_check=True)
            pe.matmul(SO[:, 0:256], kv[0:NS, 2, 384:512], pT_n[:, 1:3, :], start=True, stop=False, skip_group_check=True)
            for m in range(2):
                pe.matmul(SO[:, 256 + 64 * m:320 + 64 * m], kv[0:NS, 2, 512 + m * P:512 + (m + 1) * P],
                          pT_n[:, 0, 64 * m:64 * m + 64], stop=False, **acc)
            pv_a = pT_s[:, 7:9, :].rearrange("p v (j t) -> p v j t", j=4)
            for b in range(NB_S):
                i = NB_S + b
                pe.wait_ge(S[f"kc{i % 2}_in"], 96 * (i // 2 + 1))
                s = cslot[i % 2]
                c4 = slice(4 * b, 4 * b + 4)
                last = b == NB_S - 1
                for v in range(2):
                    r64 = slice(64 * v, 64 * v + 64)
                    pe.matmul(SO_A[r64, v, :, c4], cache_a(s)[:, r64], pv_a[:, v, :, c4], stop=last, **acc)
                for m in range(2):
                    for r in range(NKR + 2):
                        for h in range(2):
                            r64 = slice(64 * h, 64 * h + 64)
                            cols = slice(m * P + 64 * h, m * P + 64 * h + 64)
                            q = slice(64 * m + 32 * h + 4 * b, 64 * m + 32 * h + 4 * b + 4)
                            if r < NKR:
                                pe.matmul(SO_B[r64, m, h, c4], cache_b(s)[:, r, cols], pT_s[:, r, q], stop=last, **acc)
                            else:
                                ins = pe.matmul(SO_C[r64, m, h, c4], cache_c(s)[:, r - NKR, cols],
                                                pT_s[:, 2 + r, q], stop=last, **acc)
                ins.then_inc(S["s_pv_done"], 1)
            assert gate_n[0] == 24

            pe.wait_ge(S["s_o_evicted"], 1)
            for dt in range(8):
                blk = 12 + dt // 4
                if dt % 4 == 0:
                    wblk_ready(pe, blk)
                if dt >= 2:
                    pe.wait_ge(S["merged"], dt - 1)
                for br, ks in enumerate((range(0, 4), range(4, 6), range(6, 8))):
                    for k in ks:
                        ins = pe.matmul(bank(3 * (dt % 2) + br)[:, 0:TT],
                                        wblk[blk % 2][:, k, (dt % 4) * P:(dt % 4 + 1) * P], oT[:, k, :],
                                        start=(k == ks[0]), stop=(k == ks[-1]))
                ins.then_inc(S["br_done"], 1)
            pe.wait_ge(S["merged"], 8)
            for n in range(2):
                wblk_ready(pe, 14 + n)
                for t in range(3):
                    for k in range(KC):
                        ins = pe.matmul(bank(3 * n + t)[k_rows(t, k), :], hT_v[:, k, TOK0[t]:TOK0[t] + NTOK[t]],
                                        wblk[n][:, k, :], **k_group(t, k))
                    ins.then_inc(S["wout_done"], 1)

            for g in range(6):
                pe.wait_ge(S["hn_done"], 5 + g // 2 + 1)
                if g >= 2:
                    pe.wait_ge(S["tr_evicted"], TR_H + TR_Q + g - 1)
                transposes(g)
            pe.wait_ge(S["tr_evicted"], TR_H + TR_Q + 6)
            for t in range(3):
                for k in range(KC):
                    ins = pe.matmul(bank(0)[0:NTOK[t], t * NE:(t + 1) * NE], hT_v[:, k, TOK0[t]:TOK0[t] + NTOK[t]],
                                    wrt_v[:, k, :], start=(k == 0), stop=(k == KC - 1))
                ins.then_inc(S["rt_done"], 1)
            pe.wait_ge(S["rank_lhs"], 2)
            for t in range(3):
                for t2 in range(t + 1):
                    ins = pe.matmul(bank(1)[:, t * NE:(t + 1) * NE], const("tri") if t2 == t else const("ones"),
                                    r_mask[:, t2, :], start=(t2 == 0), stop=(t2 == t))
            for t in range(3):
                ins = pe.matmul(bank(1)[0:NE, 128:129], r_mask[:, t, :], const("ones")[:, 0:1],
                                start=(t == 0), stop=(t == 2))
            ins.then_inc(S["rank_done"], 1)
            pe.wait_ge(S["rank_lhs"], 3)
            pe.matmul(bank(2)[:, 0:NE], r_novT[0:NE, :], const("tri", NE)[:, 0:NE], start=True, stop=True)
            pe.matmul(bank(2)[:, NE:2 * NE], r_novT[0:NE, :], const("tri_incl", NE)[:, 0:NE],
                      start=True, stop=True).then_inc(S["ov_done"], 1)

            def gather(b):
                pe.wait_ge(S["sel_ready"], b + 1)
                for c in range(KC):
                    for t in range(3):
                        n = NTOK[t]
                        ins = pe.matmul(bank(6)[:, c * BT:(c + 1) * BT], h_v[0:n, t, c * P:(c + 1) * P],
                                        sel[0:n, t, :], start=(t == 0), stop=(t == 2))
                ins.then_inc(S["gath_done"], 1)

            def pe_block(b):
                pe.wait_ge(S["xt_ready"], b + 1)
                for k in range(KC):
                    pe.wait_ge(slice_in[k], 16 * b + 16)
                    for u in range(2):
                        for h in range(2):
                            a = k * SLOT + u * D + h * 512
                            ins = pe.matmul(bank(u)[64 * h:64 * h + 64, :], xTe[:, k, :], ring[:, a:a + 512],
                                            start=(k == 0), stop=False, skip_group_check=True)
                    ins.then_inc(S["slices_used"], 1)
                pe.wait_ge(S["selb_ready"], b + 1)
                for u in range(2):
                    for h in range(2):
                        ins = pe.matmul(bank(u)[64 * h:64 * h + 64, :], sel_b[:, :],
                                        bias3[0:96, u * D + h * 512:u * D + (h + 1) * 512], start=False, stop=True,
                                        skip_group_check=True)
                ins.then_inc(S["gu_done"], 1)
                gather(b + 1)
                for h in range(2):
                    pe.matmul(bank(5)[64 * h:64 * h + 64, :], sel_b[:, :],
                              bias3[0:96, 2 * D + h * 512:2 * D + (h + 1) * 512], start=True, stop=False,
                              skip_group_check=True)
                pe.wait_ge(S["act_ready"], b + 1)
                for q in range(4):
                    ins = pe.transpose(bank(4)[:, q * P:(q + 1) * P], act[:, q * P:(q + 1) * P], ident)
                ins.then_inc(S["at_done"], 1)
                pe.wait_ge(S["at_evicted"], b + 1)
                for kk in range(KC):
                    if kk % 2 == 0:
                        pe.wait_ge(slice_in[8 + kk // 2], 16 * b + 16)
                    for h in range(2):
                        a = (8 + kk // 2) * SLOT + (kk % 2) * D + h * 512
                        ins = pe.matmul(bank(5)[64 * h:64 * h + 64, :], aTe[:, kk % 4, (kk // 4) * 64:(kk // 4) * 64 + 64],
                                        ring[:, a:a + 512], start=False, stop=(kk == KC - 1), skip_group_check=True)
                    if kk % 2 == 1:
                        ins.then_inc(S["slices_used" if kk < KC - 1 else "y_done"], 1)

            gather(0)
            with pe.Fori(0, NE) as b:
                pe_block(b)
            pe.wait_ge(S["tables"], 1)
            n_blk = pe.value_load(r_tab[0:1, NOV:NOV + 1], min_val=NE, max_val=NBLK)
            with pe.Fori(NE, NBLK) as b:
                with pe.If(b < n_blk):
                    pe_block(b)

        @block.vector
        def _(v):
            chain = [0]
            told = {}

            def signal(ins, name):
                told[name] = told.get(name, 0) + 1
                ins.then_inc(S[name], 1)
                v.wait_ge(S[name], told[name])

            def link(ins):
                chain[0] += 1
                ins.then_inc(S["v_self"], 1)
                v.wait_ge(S["v_self"], chain[0])

            def inverse_roots(n, step, n_sumsq):
                ms, root, inv = norm_st[:, 0:n], norm_st[:, 8:8 + n], norm_st[:, 16:16 + n]
                v.wait_ge(S["sumsq"], n_sumsq)
                link(v.tensor_scalar(ms, ms, 1.0 / D, EPS, ALU.mult, ALU.add))
                signal(v.tensor_copy(root, ms), "rstd")
                v.wait_ge(S["root"], step)
                link(v.reciprocal(inv, root))
                link(v.tensor_tensor(root, inv, inv, ALU.mult))
                link(v.tensor_tensor(root, root, ms, ALU.mult))
                link(v.tensor_scalar(root, root, -0.5, 1.5, ALU.mult, ALU.add))
                signal(v.tensor_tensor(inv, inv, root, ALU.mult), "rstd")

            link(v.memset(norm_st, 1.0))
            inverse_roots(5, 1, 5)

            def evict_tr(g, seq):
                pieces, dst, gain = tr_groups[g]
                v.wait_ge(S["tr_done"], seq + 1)
                src = tr_view(g)
                if gain is None:
                    ins = v.tensor_copy(dst, src)
                else:
                    ins = v.tensor_tensor(dst, src, gain.unsqueeze(2).to_broadcast(list(src.shape)), ALU.mult)
                ins.then_inc(S["tr_evicted"], 1)

            v.wait_ge(S["small_in"], SMALL_IN)
            v.wait_ge(S["cst_in"], 16)
            for g in range(TR_H):
                evict_tr(g, g)

            for n in range(5):
                w = qkv_cols[n][1] - qkv_cols[n][0]
                v.wait_ge(S["proj_done"], 3 * n + 3)
                if n >= 2:
                    v.wait_ge(S["proj_evicted"], 3 * (n - 2) + 3)
                parts = [bank((n % 2) * 3 + 2)[NS * q:NS * q + NS, 0:w] for q in range(4)]
                acc = s_sum[n % 2][:, 0:w]
                link(v.tensor_copy(acc, parts[0]))
                for q in (1, 2):
                    link(v.tensor_tensor(acc, acc, parts[q], ALU.add))
                signal(v.tensor_tensor(acc, acc, parts[3], ALU.add), "ssum_ready")

            tmp = probs
            for t in range(3):
                v.wait_ge(S["proj_evicted"], 12 + t + 1)
                r = NTOK[t]
                cos = const("cos")[0:r, t * 8:t * 8 + 8]
                sin = const("sin")[0:r, t * 8:t * 8 + 8]
                for src, nh in ((q_tok[0:r, t, 0:1280], 20), (kv[0:r, t, 0:384], 6)):
                    hv = src.rearrange("p (h n) -> p h n", n=HD)
                    x1, x2 = hv[:, :, 0:8], hv[:, :, 8:16]
                    T = [tmp[0:r, n * 160:n * 160 + nh * 8].rearrange("p (h n) -> p h n", n=8) for n in range(4)]
                    cb = cos.unsqueeze(1).to_broadcast([r, nh, 8])
                    sbc = sin.unsqueeze(1).to_broadcast([r, nh, 8])
                    v.tensor_tensor(T[0], x1, cb, ALU.mult)
                    v.tensor_tensor(T[1], x2, sbc, ALU.mult)
                    v.tensor_tensor(T[2], x2, cb, ALU.mult)
                    link(v.tensor_tensor(T[3], x1, sbc, ALU.mult))
                    v.tensor_tensor(x1, T[0], T[1], ALU.subtract)
                    signal(v.tensor_tensor(x2, T[2], T[3], ALU.add), "rope_done")
            for n in range(TR_Q):
                evict_tr(TR_H + n, TR_H + n)

            def unit_stats(u):
                t, br, h = units[u]
                n, nk = unit_shape(u)
                src, pr = unit_psum(u), unit_probs(u)
                v.wait_ge(S["scores_done"], u + 1)
                if u >= 2:
                    v.wait_ge(S["pt_done"], u - 1)
                if br == "a":
                    mask = const("mask_a")[:, 2 * P - nk:].unsqueeze(1).to_broadcast([P, 4, nk])
                    link(v.tensor_tensor(pr, src, mask, ALU.add))
                    link(v.tensor_reduce(st(u, 0), pr, AX.X, ALU.max))
                    sk = sink_p[:, 4 * h:4 * h + 4]
                    link(v.tensor_tensor(st(u, 0), st(u, 0), sk, ALU.max))
                    link(v.tensor_scalar(st(u, 0), st(u, 0), -1.0, None, ALU.mult))
                    signal(v.tensor_tensor(st(u, 2), st(u, 0), sk, ALU.add), "stat_ready")
                elif br == "b":
                    mask = const("mask_b").rearrange("p (g k) -> p g k", k=2 * P)[:, :, 2 * P - nk:]
                    link(v.tensor_tensor(pr, src, mask, ALU.add))
                    signal(v.tensor_reduce(st(u, 0, 1), pr, AX.XY, ALU.max, negate=True), "stat_ready")
                else:
                    signal(v.tensor_reduce(st(u, 0), src, AX.X, ALU.max, negate=True), "stat_ready")

            def unit_norm(u):
                t, br, h = units[u]
                n, nk = unit_shape(u)
                pr = unit_probs(u)
                v.wait_ge(S["exp_done"], u + 1)
                if br == "a":
                    link(v.tensor_tensor(st(u, 1), st(u, 1), st(u, 2), ALU.add))
                if br == "b":
                    v.reciprocal(st(u, 2, 1), st(u, 1, 1))
                    link(v.tensor_tensor(pr[:, 0, :], pr[:, 0, :], pr[:, 1, :], ALU.add))
                    link(v.tensor_tensor(pr[:, 0, :], pr[:, 0, :], pr[:, 2, :], ALU.add))
                    v.tensor_scalar(pr[:, 0, :], pr[:, 0, :], st(u, 2, 1), None, ALU.mult).then_inc(S["p_ready"], 1)
                    return
                link(v.reciprocal(st(u, 2), st(u, 1)))
                v.tensor_tensor(pr, pr, st(u, 2).unsqueeze(2).to_broadcast([P, 4, nk]), ALU.mult).then_inc(S["p_ready"], 1)

            unit_stats(0)
            for u in range(NU):
                if u + 1 < NU:
                    unit_stats(u + 1)
                unit_norm(u)

            for b in range(NB_S):
                for gi in range(5):
                    if (5 * b + gi) % 2 == 0:
                        evict_kt(v, b, gi, v.tensor_copy, "ktv_evicted")
            v.wait_ge(S["s_scores_done"], 1)
            nb, ncc, na = s_st[:, 0:1], s_st[:, 1:2], s_st[:, 2:4]
            link(v.tensor_tensor(PR_B, SC_B, const("smask_b"), ALU.add))
            v.tensor_tensor(PR_A, SC_A, const("smask_a").unsqueeze(1).to_broadcast([P, 2, NSM_A]), ALU.add)
            v.tensor_reduce(nb, PR_B, AX.X, ALU.max, negate=True)
            link(v.tensor_reduce(ncc, SC_C, AX.X, ALU.max, negate=True))
            link(v.tensor_reduce(na, PR_A, AX.X, ALU.max))
            link(v.tensor_tensor(na, na, sink_s, ALU.max))
            link(v.tensor_scalar(na, na, -1.0, None, ALU.mult))
            signal(v.tensor_tensor(s_st[:, 8:10], na, sink_s, ALU.add), "s_stat")
            v.wait_ge(S["s_exp"], 1)
            link(v.tensor_tensor(s_st[:, 6:8], s_st[:, 6:8], s_st[:, 8:10], ALU.add))
            link(v.reciprocal(s_st[:, 12:16], s_st[:, 4:8]))
            near = PR_B[:, 0:512].rearrange("p (a s) -> p a s", s=16)[:, :, 0:4]
            link(v.tensor_tensor(PR_B[:, 384:512], PR_B[:, 384:512], PR_B[:, 1024:1152], ALU.add))
            link(v.tensor_tensor(near, near, PR_B[:, 896:1024].rearrange("p (a s) -> p a s", s=4), ALU.add))
            new = [PR_B[:, 1152 + NS * g:1152 + NS * (g + 1)] for g in range(3)]
            link(v.tensor_tensor(new[0], new[0], new[1], ALU.add))
            link(v.tensor_tensor(new[0], new[0], new[2], ALU.add))
            v.tensor_scalar(PR_B[:, 0:896], PR_B[:, 0:896], s_st[:, 12:13], None, ALU.mult)
            v.tensor_scalar(new[0], new[0], s_st[:, 12:13], None, ALU.mult)
            v.tensor_scalar(PR_C, PR_C, s_st[:, 13:14], None, ALU.mult)
            signal(v.tensor_tensor(PR_A, PR_A, s_st[:, 14:16].unsqueeze(2).to_broadcast([P, 2, NSM_A]), ALU.mult), "s_p_ready")
            v.wait_ge(S["s_pv_done"], NB_S)
            tok = slice(SEQ, TT)
            for r in range(2):
                h = slice(64 * r, 64 * r + 64)
                v.tensor_copy(oT[h, 0:4, tok], SO_A[h, r])
                v.tensor_copy(oT[h, 4:6, tok], SO_B[h, :, r, :])
                ins = v.tensor_copy(oT[h, 6:8, tok], SO_C[h, :, r, :])
            signal(ins, "s_o_evicted")

            v.wait_ge(S["bias_raw_in"], 32)
            v.wait_ge(S["out_dma"], KV_OUT)
            for part in range(3):
                dst = bias3[32 * part:32 * part + 32, :]
                link(v.tensor_copy(dst, bias_raw))
                if part < 2:
                    link(v.tensor_tensor(bias_raw, bias_raw, dst, ALU.subtract))

            for dt in range(8):
                v.wait_ge(S["br_done"], dt + 1)
                v.wait_ge(S["gates_ready"], dt + 1)
                for br in range(3):
                    ins = v.tensor_tensor(gT[:, 8 * br + dt, :], gT[:, 8 * br + dt, :],
                                          bank(3 * (dt % 2) + br)[:, 0:TT], ALU.mult)
                link(ins)
                link(v.tensor_tensor(gT[:, dt, :], gT[:, dt, :], gT[:, 8 + dt, :], ALU.add))
                v.tensor_tensor(hT_v[:, dt, :], gT[:, dt, :], gT[:, 16 + dt, :], ALU.add).then_inc(S["merged"], 1)
            for n in range(2):
                for t in range(3):
                    v.wait_ge(S["wout_done"], 3 * n + t + 1)
                    r = NTOK[t]
                    xs = x_v[0:r, t, n * 512:(n + 1) * 512]
                    ins = v.tensor_tensor(xs, xs, bank(3 * n + t)[0:r, :], ALU.add)
                    if t == 2:
                        for q in range(1, 4):
                            link(ins)
                            ins = v.tensor_tensor(xs, xs, bank(3 * n + t)[NS * q:NS * q + NS, :], ALU.add)
                    if n == 1:
                        ins.then_inc(S["x2_done"], 1)
            inverse_roots(3, 2, 8)
            for g in range(6):
                pieces, dst, _ = tr_groups[g]
                v.wait_ge(S["tr_done"], TR_H + TR_Q + g + 1)
                src = tr_view(g)
                c = 4 * (g % 2)
                v.tensor_tensor(dst, src, gain_v[:, 2, c:c + 4].unsqueeze(2).to_broadcast(list(src.shape)), ALU.mult) \
                    .then_inc(S["tr_evicted"], 1)

            link(v.memset(rt[:, 0:96], 0.0))
            for t in range(3):
                r = NTOK[t]
                v.wait_ge(S["rt_done"], 3)
                ins = v.tensor_tensor(r_lg[0:r, t, :], bank(0)[0:r, t * NE:(t + 1) * NE], b_rt[0:r, :], ALU.add)
            link(ins)
            for t in range(3):
                link(v.max(r_mx[:, t, :], r_lg[:, t, :]))
                link(v.max_index(r_ix[:, t, :], r_mx[:, t, :], r_lg[:, t, :]))
            signal(v.tensor_tensor(r_d4, r_mx[:, :, 0:4], r_mx[:, :, 0:1].to_broadcast([P, 3, 4]), ALU.subtract), "rank_lhs")
            link(v.tensor_copy(r_ixf, r_ix))
            link(v.tensor_copy(r_sum.unsqueeze(1).rearrange("p a b -> p (a b)"), const("valid")))
            link(v.tensor_copy(r_gate, r_ixf[:, :, 0:4]))
            ix12 = r_gate.rearrange("p t j -> p (t j)")
            link(v.tensor_tensor(r_oh, const("iota_e").unsqueeze(1).to_broadcast([P, 12, NE]),
                                 ix12.unsqueeze(2).to_broadcast([P, 12, NE]), ALU.is_equal))
            link(v.tensor_reduce(r_mask, r_oh.rearrange("p (t j) e -> p t e j", j=4), AX.X, ALU.add))
            signal(v.tensor_tensor(r_mask, r_mask, const("valid").unsqueeze(2).to_broadcast([P, 3, NE]), ALU.mult), "rank_lhs")
            v.wait_ge(S["nov_done"], 1)
            link(v.tensor_reduce(r_sum, r_d4, AX.X, ALU.add))
            link(v.reciprocal(r_sum, r_sum))
            link(v.tensor_tensor(r_gate, r_d4, r_sum.unsqueeze(2).to_broadcast([P, 3, 4]), ALU.mult))
            v.wait_ge(S["rank_done"], 1)
            link(v.tensor_copy(r_rank.rearrange("p t e -> p (t e)"), bank(1)[:, 0:96]))
            cnt = r_cnt[0:NE, 0:1]
            link(v.tensor_copy(cnt, bank(1)[0:NE, 128:129]))
            nov = r_cnt[0:NE, 1:2]
            link(v.tensor_scalar(nov, cnt, float(BT), None, ALU.is_gt))
            for m in range(2, (TT + BT - 1) // BT):
                link(v.tensor_scalar(r_cnt[0:NE, 2:3], cnt, float(BT * m), None, ALU.is_gt))
                link(v.tensor_tensor(nov, nov, r_cnt[0:NE, 2:3], ALU.add))
            signal(v.tensor_scalar(r_novT[0:NE, :], const("ones", NE), nov, None, ALU.mult), "rank_lhs")
            v.wait_ge(S["ov_done"], 1)
            link(v.tensor_copy(r_ovs, bank(2)[:, 0:NE]))
            link(v.tensor_copy(r_ove, bank(2)[:, NE:2 * NE]))
            link(v.tensor_scalar(r_base, r_ovs, float(BT), float(BT * (NE - 1) + 1), ALU.mult, ALU.add))
            link(v.tensor_tensor(r_base, r_base, const("e_base"), ALU.subtract))
            link(v.tensor_scalar(r_ge, r_rank, float(BT), None, ALU.is_ge))
            link(v.tensor_tensor(r_ge, r_ge, r_base.unsqueeze(1).to_broadcast([P, 3, NE]), ALU.mult))
            link(v.tensor_tensor(r_ge, r_ge, r_rank, ALU.add))
            link(v.tensor_tensor(r_ge, r_ge, const("e_base").unsqueeze(1).to_broadcast([P, 3, NE]), ALU.add))
            link(v.tensor_tensor(r_g1, r_ge, r_mask, ALU.mult))

            bcnt, ecur, ecur2 = ecols[:, 0:1], ecols[:, 1:2], ecols[:, 2:3]
            brow = ecols[:, 3:4]
            vt = ecols[:, 4:7]
            cmp_e = bsel[0]
            link(v.memset(bcnt, 0.0))
            link(v.memset(brow, 0.0))
            link(v.tensor_scalar(r_ove, r_ove, float(NE), None, ALU.add))

            def prepare(wait_own):
                wait_own(v.tensor_scalar(sel_d, r_g1.rearrange("p t e -> p (t e)"), brow, 0.0, ALU.subtract, ALU.max))
                wait_own(v.scalar_tensor_tensor(sel_d, sel_d, float(BT), sel_d, ALU.is_le, ALU.mult))
                wait_own(v.tensor_reduce(vt, sel_d.rearrange("p (t e) -> p t e", e=NE), AX.X, ALU.add))
                v.tensor_tensor(sel, const("iota_slot").unsqueeze(1).to_broadcast([P, 3, BT]),
                                vt.unsqueeze(2).to_broadcast([P, 3, BT]), ALU.is_equal).then_inc(S["sel_ready"], 1)
                wait_own(v.tensor_scalar(brow, brow, float(BT), None, ALU.add))

            def bias_rows(wait_own):
                wait_own(v.tensor_scalar(cmp_e, r_ove, bcnt, None, ALU.is_le))
                wait_own(v.tensor_reduce(ecur, cmp_e, AX.X, ALU.add))
                wait_own(v.scalar_tensor_tensor(ecur2, bcnt, float(NE), bcnt, ALU.is_lt, ALU.mult))
                wait_own(v.tensor_tensor(ecur, ecur, ecur2, ALU.add))
                wait_own(v.tensor_scalar(bcnt, bcnt, 1.0, None, ALU.add))
                v.tensor_scalar(sel_b[:, :], const("kmod", 96), ecur[0:96, :], None, ALU.is_equal) \
                    .then_inc(S["selb_ready"], 1)

            prepare(link)
            link(v.tensor_tensor(r_cmp[0:1], r_ove[0:1, :].unsqueeze(1).to_broadcast([1, NOV, NE]),
                                 const("iota_ov", 1).unsqueeze(2).to_broadcast([1, NOV, NE]), ALU.subtract))
            link(v.tensor_scalar(r_cmp[0:1], r_cmp[0:1], float(NE), None, ALU.is_le))
            link(v.tensor_reduce(r_exp[0:1, :], r_cmp[0:1], AX.X, ALU.add))
            link(v.tensor_scalar(r_exp[0:1, :], r_exp[0:1, :], float(NE - 1), None, ALU.min))
            link(v.tensor_copy(r_tab[0:1, 0:NOV], r_exp[0:1, :]))
            link(v.tensor_copy(r_tab[0:1, NOV:NOV + 1], r_ove[0:1, NE - 1:NE]))
            g4 = r_tmp.rearrange("p (t j) e -> p t j e", j=4)
            for t in range(3):
                link(v.tensor_tensor(g4[:, t], r_oh.rearrange("p (t j) e -> p t j e", j=4)[:, t],
                                     r_g1[:, t, :].unsqueeze(1).to_broadcast([P, 4, NE]), ALU.mult))
            link(v.tensor_reduce(r_idxf, r_tmp, AX.X, ALU.add))
            signal(v.tensor_scalar(r_idxf, r_idxf, 1.0, None, ALU.max), "tables")
            v.wait_ge(S["gath_done"], 1)
            gain_x = gain_v[:, 2, :].unsqueeze(2).to_broadcast([P, KC, BT])
            xps = bank(6)[:, :].rearrange("p (k s) -> p k s", s=BT)
            v.tensor_tensor(xTe, xps, gain_x, ALU.mult).then_inc(S["xt_ready"], 1)

            bias_rows(link)
            base = chain[0]
            per_block = 3 + 1 + 4 + 1 + 2

            def v_block(b):
                seen = [0]

                def own(ins):
                    seen[0] += 1
                    ins.then_inc(S["v_self"], 1)
                    v.wait_ge(S["v_self"], b * per_block + (base + seen[0]))

                v.wait_ge(S["gath_done"], b + 1)
                prepare(own)
                v.wait_ge(S["gu_done"], b + 1)
                v.tensor_scalar(g_min, bank(0), LIMIT, None, ALU.min).then_inc(S["g_ready"], 1)
                own(v.tensor_scalar(u_clip, bank(1), LIMIT, -LIMIT, ALU.min, ALU.max))
                v.wait_ge(S["g_ready"], b + 1)
                own(v.scalar_tensor_tensor(u_clip, u_clip, 1.0, g_min, ALU.add, ALU.mult))
                v.wait_ge(S["sig_ready"], b + 1)
                v.tensor_tensor(act, u_clip, g_sig, ALU.mult).then_inc(S["act_ready"], 1)
                v.wait_ge(S["gath_done"], b + 2)
                v.tensor_tensor(xTe, xps, gain_x, ALU.mult).then_inc(S["xt_ready"], 1)
                v.wait_ge(S["y_evicted"], b + 1)
                bias_rows(own)
                assert seen[0] == per_block, seen

            with v.Fori(0, NE) as b:
                v_block(b)
            n_blk = v.value_load(r_tab[0:1, NOV:NOV + 1], min_val=NE, max_val=NBLK)
            with v.Fori(NE, NBLK) as b:
                with v.If(b < n_blk):
                    v_block(b)

            for j in range(3 * TOPK):
                t = j // TOPK
                r = NTOK[t]
                v.wait_ge(S[f"gath{t}_in"], 16 * TOPK)
                if j % TOPK:
                    v.wait_ge(S["comb"], j)
                v.scalar_tensor_tensor(x_v[0:r, t, :], ring[0:r, j * D:(j + 1) * D],
                                       r_gate[0:r, t, j % TOPK:j % TOPK + 1], x_v[0:r, t, :],
                                       ALU.mult, ALU.add).then_inc(S["comb"], 1)
            tail = [0]

            def tail_link(ins):
                tail[0] += 1
                ins.then_inc(S["tail_self"], 1)
                v.wait_ge(S["tail_self"], tail[0])

            ms, root, inv = norm_st[:, 0:3], norm_st[:, 8:11], norm_st[:, 16:19]
            v.wait_ge(S["sumsq"], 11)
            tail_link(v.tensor_scalar(ms, ms, 1.0 / D, EPS, ALU.mult, ALU.add))
            signal(v.tensor_copy(root, ms), "rstd")
            v.wait_ge(S["root"], 3)
            tail_link(v.reciprocal(inv, root))
            tail_link(v.tensor_tensor(root, inv, inv, ALU.mult))
            tail_link(v.tensor_tensor(root, root, ms, ALU.mult))
            tail_link(v.tensor_scalar(root, root, -0.5, 1.5, ALU.mult, ALU.add))
            tail_link(v.tensor_tensor(inv, inv, root, ALU.mult))
            v.wait_ge(S["gain_in"], 16)
            for t in range(3):
                r = NTOK[t]
                v.scalar_tensor_tensor(x_v[0:r, t, :], x_v[0:r, t, :], inv[0:r, t:t + 1], g_final[0:r, :],
                                       ALU.mult, ALU.mult).then_inc(S["fin_done"], 1)


_INS = ['x_prompt', 'x_sample', 'cache_swa_k', 'cache_swa_v', 'cache_dil_k', 'cache_dil_v', 'cache_mem_k',
        'cache_mem_v', 'mem_prompt', 'norm_attn', 'norm_mem', 'w_in', 'w_mem_kv', 'sinks', 'w_br_a', 'w_br_b',
        'w_br_c', 'w_out', 'norm_ffn', 'w_router', 'b_router', 'w_gate_up', 'b_gate_up', 'w_down', 'b_down',
        'norm_final']
_OUTS = [('y_p', (1, SEQ, D)), ('y_s', (NB_S, NQ_S, D)),
         ('swa_k_p', (1, 1, LA, 2, HD)), ('swa_v_p', (1, 1, LA, 2, HD)),
         ('dil_k_p', (1, 1, SEQ, 4, HD)), ('dil_v_p', (1, 1, SEQ, 4, HD)),
         ('mem_k_p', (1, 1, LM, 4, HD)), ('mem_v_p', (1, 1, LM, 4, HD)),
         ('swa_k_s', (1, NB_S, LA, 2, HD)), ('swa_v_s', (1, NB_S, LA, 2, HD)),
         ('dil_k_s', (1, NB_S, LB, 4, HD)), ('dil_v_s', (1, NB_S, LB, 4, HD))]


def kernel(**inputs):
    import concourse.bacc as bacc
    from concourse.bass_utils import run_bass_kernel_spmd

    nc = bacc.Bacc("TRN2", target_bir_lowering=False, num_devices=1)
    arrays, d = {}, {}
    for name in _INS:
        a = np.ascontiguousarray(inputs[name])
        arrays["in_" + name] = a
        d[name] = nc.dram_tensor("in_" + name, a.shape, mybir.dt.from_np(a.dtype), kind="ExternalInput").ap()
    table, _ = constants()
    arrays["in_consts"] = table
    d["consts"] = nc.dram_tensor("in_consts", table.shape, F32, kind="ExternalInput").ap()
    for name, shape in _OUTS:
        d[name] = nc.dram_tensor("out_" + name, shape, F32, kind="ExternalOutput").ap()
    build(nc, d)
    r = run_bass_kernel_spmd(nc, [arrays], core_ids=[0])
    return tuple(r.results[0]["out_" + name] for name, _ in _OUTS)
```
